# Optimizing a Trainium2 kernel written in Bass

```python
import jax, jax.numpy as jnp
from jax import lax
import numpy as np

D_MODEL = 1024
BATCH = 1
SEQ = 256
DEPTH = 1

D_MIX = D_MODEL
HG_HEADS = 4
HG_DK = 128
HG_DV = 128
HG_WIDTH = HG_HEADS * HG_DV
HG_CHUNK = 64
SA_HEADS = 4
SA_HEAD_DIM = 64
SA_WIDTH = SA_HEADS * SA_HEAD_DIM
IDX_HEADS = 8
IDX_DIM = 32
IDX_TOPK_MAX = 256
IDX_TOPK_DIV = 4
Q_BLOCK = 128
CV_WIDTH = D_MIX - HG_WIDTH - SA_WIDTH
CV_WIDTH_FILTER = 31
D_FF = 4 * D_MODEL
N_MOD = 6
EPS = 1e-6
NEG_BIG = -1e30
TINY = 1e-30

IN_SIZES = (
    HG_HEADS * HG_DK,
    HG_HEADS * HG_DK,
    HG_WIDTH,
    HG_WIDTH,
    SA_WIDTH,
    SA_WIDTH,
    SA_WIDTH,
    IDX_HEADS * IDX_DIM,
    IDX_DIM,
    IDX_HEADS,
    2 * CV_WIDTH,
)
D_IN = sum(IN_SIZES)


def rmsnorm(x, w):
    xf = x.astype(jnp.float32)
    y = xf * lax.rsqrt(jnp.mean(xf * xf, axis=-1, keepdims=True) + EPS)
    return (y * w.astype(jnp.float32)).astype(x.dtype)

def hgrn2_lower_bounds(lb_logits):
    p = jax.nn.softmax(lb_logits.astype(jnp.float32), axis=0)
    return jnp.cumsum(p, axis=0) - p[0]

def hgrn2_mixer(q_raw, f_raw, i_in, g_raw, lb, onorm_w):
    f32 = jnp.float32
    dt = q_raw.dtype
    bsz, L, _ = q_raw.shape
    lb = lb.astype(f32)
    fr = f_raw.astype(f32)
    q = jax.nn.silu(q_raw.astype(f32)) * (HG_DK ** -0.5)
    f = lb + (1.0 - lb) * jax.nn.sigmoid(fr)
    log_f = jnp.log(jnp.maximum(f, TINY))
    k = (1.0 - lb) * jax.nn.sigmoid(-fr)
    v = i_in.astype(f32)
    n_chunks = L // HG_CHUNK

    def to_chunks(t, d):
        return t.reshape(bsz, n_chunks, HG_CHUNK, HG_HEADS, d).transpose(1, 0, 3, 2, 4)

    causal = jnp.tril(jnp.ones((HG_CHUNK, HG_CHUNK), dtype=bool))

    def step(S, xs):
        qc, kc, gc, vc = xs
        G = jnp.cumsum(gc, axis=-2)
        o_inter = jnp.einsum('bhik,bhkv->bhiv', qc * jnp.exp(G), S)
        diff = G[:, :, :, None, :] - G[:, :, None, :, :]
        decay = jnp.exp(jnp.where(causal[:, :, None], diff, NEG_BIG))
        A = jnp.einsum('bhik,bhijk,bhjk->bhij', qc, decay, kc)
        o_intra = jnp.einsum('bhij,bhjv->bhiv', A, vc)
        G_last = G[:, :, -1:, :]
        S_new = jnp.exp(G_last[:, :, 0, :])[..., None] * S + jnp.einsum(
            'bhjk,bhjv->bhkv', kc * jnp.exp(G_last - G), vc)
        return S_new, o_inter + o_intra

    S0 = jnp.zeros((bsz, HG_HEADS, HG_DK, HG_DV), f32)
    _, o = lax.scan(step, S0, (to_chunks(q, HG_DK), to_chunks(k, HG_DK),
                               to_chunks(log_f, HG_DK), to_chunks(v, HG_DV)))
    o = o.transpose(1, 0, 3, 2, 4).reshape(bsz, L, HG_HEADS, HG_DV)
    o = o * lax.rsqrt(jnp.mean(o * o, axis=-1, keepdims=True) + EPS)
    o = o * onorm_w.astype(f32).reshape(HG_HEADS, HG_DV)
    o = o.reshape(bsz, L, HG_WIDTH) * jax.nn.silu(g_raw.astype(f32))
    return o.astype(dt)

def dsa_mixer(q, k, v, q_idx, k_idx, w_idx):
    f32 = jnp.float32
    dt = q.dtype
    bsz, L, _ = q.shape
    topk = min(IDX_TOPK_MAX, L // IDX_TOPK_DIV)
    n_blk = L // Q_BLOCK
    q = q.reshape(bsz, L, SA_HEADS, SA_HEAD_DIM)
    k = k.reshape(bsz, L, SA_HEADS, SA_HEAD_DIM)
    v = v.reshape(bsz, L, SA_HEADS, SA_HEAD_DIM)
    q_idx = q_idx.reshape(bsz, L, IDX_HEADS, IDX_DIM)
    w_idx = w_idx.astype(f32) * (IDX_HEADS ** -0.5)
    k_idx_f = k_idx.astype(f32)
    key_pos = jnp.arange(L, dtype=jnp.int32)

    def blocks(t):
        return t.reshape(bsz, n_blk, Q_BLOCK, *t.shape[2:]).swapaxes(0, 1)

    def one_block(xs):
        qb, qib, wb, t0 = xs
        qpos = t0 + jnp.arange(Q_BLOCK, dtype=jnp.int32)
        s = jnp.einsum('bqhd,bsd->bqhs', qib.astype(f32), k_idx_f) * (IDX_DIM ** -0.5)
        score = jnp.einsum('bqh,bqhs->bqs', wb, jax.nn.relu(s))
        admissible = key_pos[None, :] <= qpos[:, None]
        score = jnp.where(admissible[None], score, NEG_BIG)
        _, sel = lax.top_k(score, topk)
        valid = sel <= qpos[None, :, None]
        kg = jax.vmap(lambda kk, ii: kk[ii])(k, sel)
        vg = jax.vmap(lambda vv, ii: vv[ii])(v, sel)
        logits = jnp.einsum('bqhd,bqkhd->bqhk', qb.astype(f32), kg.astype(f32)) * (SA_HEAD_DIM ** -0.5)
        logits = jnp.where(valid[:, :, None, :], logits, NEG_BIG)
        p = jax.nn.softmax(logits, axis=-1)
        o = jnp.einsum('bqhk,bqkhd->bqhd', p, vg.astype(f32))
        return o.reshape(bsz, Q_BLOCK, SA_WIDTH).astype(dt)

    t0s = jnp.arange(n_blk, dtype=jnp.int32) * Q_BLOCK
    out = lax.map(one_block, (blocks(q), blocks(q_idx), blocks(w_idx), t0s))
    return out.swapaxes(0, 1).reshape(bsz, L, SA_WIDTH)

def conv_module(u, cv_w, cv_b, ln_w, ln_b):
    f32 = jnp.float32
    dt = u.dtype
    a, b = jnp.split(u, 2, axis=-1)
    h = a * jax.nn.sigmoid(b)
    h = lax.conv_general_dilated(
        h, cv_w[:, None, :], window_strides=(1,),
        padding=[(CV_WIDTH_FILTER - 1, 0)],
        dimension_numbers=('NWC', 'WIO', 'NWC'),
        feature_group_count=CV_WIDTH) + cv_b
    hf = h.astype(f32)
    mu = jnp.mean(hf, axis=-1, keepdims=True)
    var = jnp.mean(jnp.square(hf - mu), axis=-1, keepdims=True)
    hf = (hf - mu) * lax.rsqrt(var + EPS) * ln_w.astype(f32) + ln_b.astype(f32)
    return jax.nn.silu(hf).astype(dt)

def first_inputs(seed: int = 0) -> dict:
    key = jax.random.key(seed)
    ks = jax.random.split(key, 17)
    f32 = jnp.float32
    n = lambda k, shape, s: jax.random.normal(k, shape, f32) * s
    return {
        "x": n(ks[0], (BATCH, SEQ, D_MODEL), 1.0),
        "c": n(ks[1], (BATCH, D_MODEL), 1.0),
        "ada_w": n(ks[2], (DEPTH, D_MODEL, N_MOD * D_MODEL), 0.5 * D_MODEL ** -0.5),
        "ada_b": n(ks[3], (DEPTH, N_MOD * D_MODEL), 0.02),
        "norm_mix_w": 1.0 + n(ks[4], (DEPTH, D_MODEL), 0.05),
        "norm_mlp_w": 1.0 + n(ks[5], (DEPTH, D_MODEL), 0.05),
        "w_in": n(ks[6], (DEPTH, D_MODEL, D_IN), D_MODEL ** -0.5),
        "hg_lb_logits": n(ks[7], (DEPTH, HG_HEADS * HG_DK), 1.0),
        "hg_onorm_w": 1.0 + n(ks[8], (DEPTH, HG_WIDTH), 0.05),
        "cv_w": n(ks[9], (DEPTH, CV_WIDTH_FILTER, CV_WIDTH), CV_WIDTH_FILTER ** -0.5),
        "cv_b": n(ks[10], (DEPTH, CV_WIDTH), 0.02),
        "cv_ln_w": 1.0 + n(ks[11], (DEPTH, CV_WIDTH), 0.05),
        "cv_ln_b": n(ks[12], (DEPTH, CV_WIDTH), 0.02),
        "w_out": n(ks[13], (DEPTH, D_MIX, D_MODEL), D_MIX ** -0.5),
        "mlp_w1": n(ks[14], (DEPTH, D_MODEL, D_FF), D_MODEL ** -0.5),
        "mlp_w2": n(ks[15], (DEPTH, D_FF, D_MODEL), D_FF ** -0.5),
        "final_norm_w": 1.0 + n(ks[16], (D_MODEL,), 0.05),
    }

def first_block(x, c, ada_w, ada_b, norm_mix_w, norm_mlp_w, w_in, hg_lb_logits, hg_onorm_w,
              cv_w, cv_b, cv_ln_w, cv_ln_b, w_out, mlp_w1, mlp_w2, final_norm_w):
    offsets = np.cumsum(IN_SIZES)[:-1].tolist()
    lower_bounds = hgrn2_lower_bounds(hg_lb_logits)
    c_act = jax.nn.silu(c)
    for l in range(DEPTH):
        mod = c_act @ ada_w[l] + ada_b[l]
        sh1, sc1, g1, sh2, sc2, g2 = [m[:, None, :] for m in jnp.split(mod, N_MOD, axis=-1)]

        h = rmsnorm(x, norm_mix_w[l]) * (1.0 + sc1) + sh1
        proj = h @ w_in[l]
        (hq, hf, hi, hg, sq, sk, sv, iq, ik, iw, cu) = jnp.split(proj, offsets, axis=-1)
        o_a = hgrn2_mixer(hq, hf, hi, hg, lower_bounds[l], hg_onorm_w[l])
        o_b = dsa_mixer(sq, sk, sv, iq, ik, iw)
        o_c = conv_module(cu, cv_w[l], cv_b[l], cv_ln_w[l], cv_ln_b[l])
        mix = jnp.concatenate([o_a, o_b, o_c], axis=-1) @ w_out[l]
        x = x + g1 * mix

        h = rmsnorm(x, norm_mlp_w[l]) * (1.0 + sc2) + sh2
        ff = jnp.square(jax.nn.relu(h @ mlp_w1[l])) @ mlp_w2[l]
        x = x + g2 * ff
    return rmsnorm(x, final_norm_w)


DEPTH_2 = 2

CHUNK = 64
P_DIM = 256
MLA_HEADS = 8
MLA_NOPE = 64
MLA_ROPE = 32
MLA_V = 64
Q_LORA = 256
KV_LORA = 256
ROPE_BASE = 10000.0
SB_HEADS = 8
SB_DIM = 64
FOX_HEADS = 16
FOX_DIM = 64
D_FF_2 = ((-(-8 * D_MODEL // 3)) + 255) // 256 * 256
DEEPNORM_ALPHA = (2.0 * DEPTH_2) ** 0.25
DEEPNORM_BETA = (8.0 * DEPTH_2) ** -0.25
N_EVEN = (DEPTH_2 + 1) // 2
N_ODD = DEPTH_2 // 2
IN_A = Q_LORA + KV_LORA + MLA_ROPE
IN_B = 3 * SB_HEADS * SB_DIM
IN_C = 3 * FOX_HEADS * FOX_DIM + FOX_HEADS
MIX_A = MLA_HEADS * MLA_V + SB_HEADS * SB_DIM
MIX_C = FOX_HEADS * FOX_DIM


def layer_norm(x, g, b, eps=1e-5):
    xf = x.astype(jnp.float32)
    mu = jnp.mean(xf, -1, keepdims=True)
    var = jnp.mean(jnp.square(xf - mu), -1, keepdims=True)
    return ((xf - mu) * lax.rsqrt(var + eps) * g + b).astype(x.dtype)

def rms_norm(x, g, eps=1e-6):
    xf = x.astype(jnp.float32)
    return (xf * lax.rsqrt(jnp.mean(jnp.square(xf), -1, keepdims=True) + eps) * g).astype(x.dtype)

def rope_tables(seq, dim):
    inv = 1.0 / (ROPE_BASE ** (jnp.arange(0, dim, 2, dtype=jnp.float32) / dim))
    ang = jnp.arange(seq, dtype=jnp.float32)[:, None] * inv[None, :]
    return jnp.cos(ang), jnp.sin(ang)

def apply_rope(x, cos, sin):
    x1, x2 = jnp.split(x, 2, axis=-1)
    return jnp.concatenate([x1 * cos - x2 * sin, x1 * sin + x2 * cos], -1).astype(x.dtype)

def sweep_query_blocks(block_fn, q):
    b, h, s, d = q.shape
    nb = s // Q_BLOCK
    q_blocks = q.reshape(b, h, nb, Q_BLOCK, d).transpose(2, 0, 1, 3, 4)
    out = lax.map(lambda a: block_fn(a[0], a[1]), (q_blocks, jnp.arange(nb)))
    dv = out.shape[-1]
    return out.transpose(1, 0, 3, 2, 4).reshape(b, s, h * dv)

def mla_block(q_blk, blk, k, v):
    t = blk * Q_BLOCK + jnp.arange(Q_BLOCK)
    s = jnp.arange(k.shape[2])
    allowed = (s[None, :] // CHUNK) <= (t[:, None] // CHUNK)
    logits = jnp.einsum('bhqd,bhkd->bhqk', q_blk, k).astype(jnp.float32) * (MLA_NOPE + MLA_ROPE) ** -0.5
    w = jax.nn.softmax(jnp.where(allowed, logits, -jnp.inf), axis=-1)
    return jnp.einsum('bhqk,bhkd->bhqd', w.astype(v.dtype), v)

def stick_breaking_block(q_blk, blk, k, v):
    t = blk * Q_BLOCK + jnp.arange(Q_BLOCK)
    s = jnp.arange(k.shape[2])
    past = s[None, :] < t[:, None]
    z = jnp.einsum('bhqd,bhkd->bhqk', q_blk, k).astype(jnp.float32) * SB_DIM ** -0.5
    log_beta = jax.nn.log_sigmoid(z)
    log_rem = jnp.where(past, jax.nn.log_sigmoid(-z), 0.0)
    between = lax.cumsum(log_rem, axis=3, reverse=True) - log_rem
    att = jnp.where(past, jnp.exp(log_beta + between), 0.0)
    return jnp.einsum('bhqk,bhkd->bhqd', att.astype(v.dtype), v)

def forgetting_block(q_blk, blk, k, v, dcum):
    t = blk * Q_BLOCK + jnp.arange(Q_BLOCK)
    s = jnp.arange(k.shape[2])
    causal = s[None, :] <= t[:, None]
    d_t = lax.dynamic_slice_in_dim(dcum, blk * Q_BLOCK, Q_BLOCK, axis=2)
    logits = (jnp.einsum('bhqd,bhkd->bhqk', q_blk, k).astype(jnp.float32) * FOX_DIM ** -0.5
              + d_t[..., :, None] - dcum[..., None, :])
    w = jax.nn.softmax(jnp.where(causal, logits, -jnp.inf), axis=-1)
    return jnp.einsum('bhqk,bhkd->bhqd', w.astype(v.dtype), v)

def mixer_mla_sb(x, w_in, q_norm_g, w_uq, kv_norm_g, w_ukv, w_out, cos, sin):
    b, s, _ = x.shape
    h = x @ w_in
    c_q, c_kv, k_rope, sb_qkv = jnp.split(h, [Q_LORA, Q_LORA + KV_LORA, IN_A], axis=-1)
    q = (rms_norm(c_q, q_norm_g) @ w_uq).reshape(b, s, MLA_HEADS, MLA_NOPE + MLA_ROPE).transpose(0, 2, 1, 3)
    q_nope, q_rope = jnp.split(q, [MLA_NOPE], axis=-1)
    q = jnp.concatenate([q_nope, apply_rope(q_rope, cos, sin)], -1)
    kv = (rms_norm(c_kv, kv_norm_g) @ w_ukv).reshape(b, s, MLA_HEADS, MLA_NOPE + MLA_V).transpose(0, 2, 1, 3)
    k_nope, v_a = jnp.split(kv, [MLA_NOPE], axis=-1)
    k_rope = apply_rope(k_rope[:, None], cos, sin)
    k_a = jnp.concatenate([k_nope, jnp.broadcast_to(k_rope, (b, MLA_HEADS, s, MLA_ROPE))], -1)
    o_a = sweep_query_blocks(lambda qb, i: mla_block(qb, i, k_a, v_a), q)
    q_b, k_b, v_b = sb_qkv.reshape(b, s, 3, SB_HEADS, SB_DIM).transpose(2, 0, 3, 1, 4)
    o_b = sweep_query_blocks(lambda qb, i: stick_breaking_block(qb, i, k_b, v_b), q_b)
    return jnp.concatenate([o_a, o_b], -1) @ w_out

def mixer_fox(x, w_in, b_f, w_out):
    b, s, _ = x.shape
    h = x @ w_in
    qkv, f_logit = jnp.split(h, [3 * FOX_HEADS * FOX_DIM], axis=-1)
    q, k, v = qkv.reshape(b, s, 3, FOX_HEADS, FOX_DIM).transpose(2, 0, 3, 1, 4)
    log_f = jax.nn.log_sigmoid((f_logit + b_f).astype(jnp.float32))
    dcum = lax.cumsum(log_f, axis=1).transpose(0, 2, 1)
    o = sweep_query_blocks(lambda qb, i: forgetting_block(qb, i, k, v, dcum), q)
    return o @ w_out

def swiglu(x, w1, w3, w2):
    return (jax.nn.silu(x @ w1) * (x @ w3)) @ w2

def second_inputs(seed: int = 0) -> dict:
    key = jax.random.key(seed)
    ks = iter(jax.random.split(key, 32))

    def dense(shape, fan_in, scale=1.0):
        return jax.random.normal(next(ks), shape, jnp.float32) * (fan_in ** -0.5) * scale

    def gain(shape):
        return 1.0 + 0.02 * jax.random.normal(next(ks), shape, jnp.float32)

    def bias(shape):
        return 0.02 * jax.random.normal(next(ks), shape, jnp.float32)

    return {
        "x": jax.random.normal(next(ks), (BATCH, SEQ, D_MODEL), jnp.float32),
        "p": jax.random.normal(next(ks), (DEPTH_2, BATCH, SEQ, P_DIM), jnp.float32),
        "a_w_in": dense((N_EVEN, D_MODEL, IN_A + IN_B), D_MODEL),
        "a_q_norm": gain((N_EVEN, Q_LORA)),
        "a_w_uq": dense((N_EVEN, Q_LORA, MLA_HEADS * (MLA_NOPE + MLA_ROPE)), Q_LORA),
        "a_kv_norm": gain((N_EVEN, KV_LORA)),
        "a_w_ukv": dense((N_EVEN, KV_LORA, MLA_HEADS * (MLA_NOPE + MLA_V)), KV_LORA),
        "a_w_out": dense((N_EVEN, MIX_A, D_MODEL), MIX_A, DEEPNORM_BETA),
        "c_w_in": dense((N_ODD, D_MODEL, IN_C), D_MODEL),
        "c_b_f": jax.random.uniform(next(ks), (N_ODD, FOX_HEADS), jnp.float32, 1.0, 4.0),
        "c_w_out": dense((N_ODD, MIX_C, D_MODEL), MIX_C, DEEPNORM_BETA),
        "ffn_w1": dense((DEPTH_2, D_MODEL, D_FF_2), D_MODEL),
        "ffn_w3": dense((DEPTH_2, D_MODEL, D_FF_2), D_MODEL),
        "ffn_w2": dense((DEPTH_2, D_FF_2, D_MODEL), D_FF_2, DEEPNORM_BETA),
        "ln1_g": gain((DEPTH_2, D_MODEL)),
        "ln1_b": bias((DEPTH_2, D_MODEL)),
        "ln2_g": gain((DEPTH_2, D_MODEL)),
        "ln2_b": bias((DEPTH_2, D_MODEL)),
        "ple_w_proj": dense((DEPTH_2, P_DIM, D_MODEL), P_DIM),
        "ple_w_gate": dense((DEPTH_2, D_MODEL, D_MODEL), D_MODEL),
        "ple_b_gate": bias((DEPTH_2, D_MODEL)),
    }

def second_block(x, p, a_w_in, a_q_norm, a_w_uq, a_kv_norm, a_w_ukv, a_w_out,
              c_w_in, c_b_f, c_w_out, ffn_w1, ffn_w3, ffn_w2,
              ln1_g, ln1_b, ln2_g, ln2_b, ple_w_proj, ple_w_gate, ple_b_gate):
    cos, sin = rope_tables(x.shape[1], MLA_ROPE)
    for i in range(DEPTH_2):
        j = i // 2
        if i % 2 == 0:
            mix = mixer_mla_sb(x, a_w_in[j], a_q_norm[j], a_w_uq[j], a_kv_norm[j],
                               a_w_ukv[j], a_w_out[j], cos, sin)
        else:
            mix = mixer_fox(x, c_w_in[j], c_b_f[j], c_w_out[j])
        x = layer_norm(DEEPNORM_ALPHA * x + mix, ln1_g[i], ln1_b[i])
        x = layer_norm(DEEPNORM_ALPHA * x + swiglu(x, ffn_w1[i], ffn_w3[i], ffn_w2[i]), ln2_g[i], ln2_b[i])
        x = x + jax.nn.sigmoid(x @ ple_w_gate[i] + ple_b_gate[i]) * (p[i] @ ple_w_proj[i])
    return x


def setup_inputs(seed=0):
    out = dict(first_inputs(seed))
    for name, value in second_inputs(seed + 1).items():
        if name != "x":
            out[name + "_2"] = value
    return out


def reference(
    x, c, ada_w, ada_b, norm_mix_w, norm_mlp_w, w_in, hg_lb_logits, hg_onorm_w, cv_w, cv_b,
    cv_ln_w, cv_ln_b, w_out, mlp_w1, mlp_w2, final_norm_w, p_2, a_w_in_2, a_q_norm_2, a_w_uq_2,
    a_kv_norm_2, a_w_ukv_2, a_w_out_2, c_w_in_2, c_b_f_2, c_w_out_2, ffn_w1_2, ffn_w3_2,
    ffn_w2_2, ln1_g_2, ln1_b_2, ln2_g_2, ln2_b_2, ple_w_proj_2, ple_w_gate_2, ple_b_gate_2,
):
    x = first_block(
        x, c, ada_w, ada_b, norm_mix_w, norm_mlp_w, w_in, hg_lb_logits, hg_onorm_w, cv_w, cv_b,
        cv_ln_w, cv_ln_b, w_out, mlp_w1, mlp_w2, final_norm_w,
    )
    return second_block(
        x, p_2, a_w_in_2, a_q_norm_2, a_w_uq_2, a_kv_norm_2, a_w_ukv_2, a_w_out_2, c_w_in_2,
        c_b_f_2, c_w_out_2, ffn_w1_2, ffn_w3_2, ffn_w2_2, ln1_g_2, ln1_b_2, ln2_g_2, ln2_b_2,
        ple_w_proj_2, ple_w_gate_2, ple_b_gate_2,
    )


_drawn_inputs = setup_inputs


def setup_inputs(seed=0):
    import zlib

    import numpy as np

    out = dict(_drawn_inputs(seed))
    spreads = {}
    factors = {'norm_mix_w': 5.028,
     'norm_mlp_w': 2.863,
     'hg_onorm_w': 8.0,
     'cv_b': 8.0,
     'cv_ln_w': 8.0,
     'cv_ln_b': 25.983,
     'a_q_norm_2': 8.0,
     'a_kv_norm_2': 8.0,
     'ple_b_gate_2': 8.0}
    for name, (base, spread) in spreads.items():
        noise = np.random.default_rng([zlib.crc32(name.encode()), seed]).standard_normal(out[name].shape)
        drawn = base * np.exp(spread * noise) if base else spread * noise
        out[name] = __import__('jax').numpy.asarray(drawn.astype(out[name].dtype))
    for name, factor in factors.items():
        out[name] = (out[name] * factor).astype(out[name].dtype)
    return out
```

```python
import concourse.bass as bass
from concourse import mybir
from contextlib import ExitStack

F32 = mybir.dt.float32
ALU = mybir.AluOpType
ACT = mybir.ActivationFunctionType
AX = mybir.AxisListType

P = 128
T = 256
TT = T // P
D = 1024
DC = D // P
TILE = 4096
SLOTS = 4
BANKS = 8
D_FF = 4096
D_FF_2 = 2816
ALPHA = 4.0 ** 0.25
EPS = 1e-6
EPS_LN = 1e-5
NEG = -1e30
TINY = 1e-30
TOPK = 64
LEVELS = [1, 2, 4, 8, 16, 32, 64]
LN_SPLIT = 2.0 ** 64

FF2_TILES = [4, 4, 4, 4, 4, 2]


def stream_names():
    names = [f"ada{i}" for i in range(4)]
    names += ["hf", "hq", "cu", "sviq", "sqk", "hg", "hi"]
    names += [f"ada{i}" for i in range(4, 12)]
    names += ["wo0", "wo1"] + [f"m1_{i}" for i in range(8)] + [f"m2_{i}" for i in range(8)]
    for layer in range(2):
        if layer == 0:
            names += ["cqkv", "sbq", "sbk", "sbv", "lora"]
        else:
            names += ["fq0", "fq1", "fk0", "fk1", "fv0", "fv1"]
        names += [f"o{layer}_{i}" for i in range(2)]
        names += [f"f13_{layer}_{i}" for i in range(11)]
        names += [f"f2_{layer}_{i}" for i in range(6)]
        names += [f"pp{layer}"] + [f"pg{layer}_{i}" for i in range(2)]
    return names


STREAM = stream_names()
TILE_NO = {n: i for i, n in enumerate(STREAM)}

PCOL = {}


def _columns():
    at = 0
    for name, n in [("c", 8), ("ada_b", 48), ("mix_w", 8), ("mlp_w", 8), ("lb", 4), ("onorm", 4),
                    ("cv_b", 2), ("cv_ln_w", 2), ("cv_ln_b", 2), ("cv_w", 62), ("fin_w", 8),
                    ("q_norm", 2), ("kv_norm", 2), ("ln1_g0", 8), ("ln1_b0", 8), ("ln2_g0", 8),
                    ("ln2_b0", 8), ("ln1_g1", 8), ("ln1_b1", 8), ("ln2_g1", 8), ("ln2_b1", 8),
                    ("b_f", 1)]:
        PCOL[name] = at
        at += n
    return at


N_PCOL = _columns()

CONST = {}


def _constants():
    at = 0
    for name, n in [("ident", 128), ("causal", 256), ("strict", 256), ("chunk", 256),
                    ("levels", 128 * len(LEVELS)), ("cos", 32), ("sin", 32), ("negsel", 16)]:
        CONST[name] = at
        at += n
    return at


N_CONST = _constants()
N_SMALL = DC * 136 + DC * 16 + DC * 32



def units(heads):
    return [(g, par, t) for g in range(heads // 4) for t in range(TT) for par in range(2)]


def unit_order(name, n):
    order = []
    for i in range(n + 2):
        if i < n:
            order.append((name, "L", i))
        if 0 <= i - 1 < n:
            order.append((name, "T", i - 1))
        if 0 <= i - 2 < n:
            order.append((name, "O", i - 2))
    return order


def psum_plan():
    plan = [("mod", 0)]

    def transposes(stage):
        plan.extend([("tr", stage, j) for j in range(4)])

    def gemm(name):
        plan.extend([(name, 0), (name, 1)])

    def level(lv):
        plan.extend([("lev", lv, 0), ("lev", lv, 1)])

    transposes("mix")
    gemm("hf")
    gemm("hq")
    gemm("cu")
    plan.append(("sv",))
    plan.append(("iq",))
    plan.extend([("ik",), ("iw",)])
    level(0)
    level(1)
    gemm("sqk")
    level(2)
    level(3)
    gemm("hg")
    level(4)
    level(5)
    gemm("hi")
    level(6)
    level(7)
    plan.append(("lev", 8, 0))
    plan.extend([("sc", t, j) for t in range(TT) for j in range(4)])
    plan.append(("mod", 1))
    plan.extend([("hgo", 0), ("hgo", 1)])
    plan.extend([("grow", 0, 0), ("grow", 0, 1)])
    plan.append(("cmean",))
    plan.append(("cvar",))
    plan.extend([("hgt", 0), ("hgt", 1)])
    plan.extend(unit_order("dsa", 4))
    gemm("wo0")
    gemm("wo1")
    transposes("mlp")
    for i in range(8):
        gemm(f"m1_{i}")
    plan.extend([("grow", 1, 0), ("grow", 1, 1)])
    plan.extend([("m2", t, n) for t in range(TT) for n in range(2)])
    transposes("fin")
    for layer in range(2):
        if layer == 0:
            gemm("cqkv")
            plan.append(("kr",))
            gemm("sbq")
            gemm("sbk")
            gemm("sbv")
            plan.extend([("ct", 0), ("ct", 1)])
            plan.extend([("uq", t, n) for t in range(TT) for n in range(2)])
            plan.extend([("uk", j) for j in range(4)])
            plan.extend([("uv", t) for t in range(TT)])
            plan.append(("krt",))
            plan.extend(unit_order("sb", 8))
            plan.extend([("qt", j) for j in range(4)])
            plan.extend(unit_order("mla", 8))
        else:
            plan.append(("ff",))
            for n in ["fq0", "fq1", "fk0", "fk1", "fv0", "fv1"]:
                gemm(n)
            plan.append(("fd",))
            plan.extend(unit_order("fox", 16))
        gemm(f"o{layer}_0")
        gemm(f"o{layer}_1")
        transposes(f"ln1_{layer}")
        for i in range(11):
            gemm(f"f13_{layer}_{i}")
        plan.extend([("f2", layer, t, n) for t in range(TT) for n in range(2)])
        transposes(f"ln2_{layer}")
        plan.extend([("pp", layer, n, t) for n in range(2) for t in range(TT)])
        gemm(f"pg{layer}_0")
        gemm(f"pg{layer}_1")
        if layer == 0:
            transposes("ple")
    return plan


PLAN = psum_plan()
USE = {key: i for i, key in enumerate(PLAN)}
assert len(USE) == len(PLAN)


def full(*key):
    return USE[key] + 1


def bank(*key):
    return USE[key] % BANKS


def read(*key):
    return USE[key] // BANKS + 1


def build(nc, x_in, wstream, wsmall, pcol_in, prow_in, const_in, p_in, out):
    ctx = ExitStack()
    with ctx:
        def sb(name, shape):
            return ctx.enter_context(nc.sbuf_tensor(name, shape, F32))

        def sem(name):
            return ctx.enter_context(nc.semaphore(name))

        ring = sb("ring", [P, SLOTS, TILE])
        x = sb("x_res", [P, TT, D])
        xn = sb("xn", [P, TT, D])
        hT = sb("hT", [P, DC, T])
        mixT = sb("mixT", [P, DC, T])
        rows = sb("rows", [P, 2, D])
        pcol = sb("pcol_sb", [P, N_PCOL])
        const = sb("const_sb", [P, N_CONST])
        small = sb("small", [P, N_SMALL])
        pT = sb("pT", [P, 2, 2, T])
        ones = sb("ones", [P, T])
        avg = sb("avg", [P, P])
        tiny = sb("tiny", [P, 256])
        ARENA = 20300
        arena = sb("arena", [P, ARENA])

        top = [0]

        def cut(n):
            a = arena[:, top[0]:top[0] + n]
            top[0] += n
            assert top[0] <= ARENA, top[0]
            return a

        psum = [ctx.enter_context(nc.psum_tensor(f"bank{i}", [P, 512], F32)) for i in range(BANKS)]

        def ps(*key):
            return psum[bank(*key)]

        def col(name, i=0, n=1):
            return pcol[:, PCOL[name] + i:PCOL[name] + i + n]

        ident = const[:, CONST["ident"]:CONST["ident"] + P]

        def bias_of(kind, t):
            at = CONST[kind]
            return const[:, at + P:at + 2 * P] if t == 0 else const[:, at:at + 2 * P]

        unit_logits = [cut(512) for _ in range(3)]
        unit_probsT = [cut(512) for _ in range(2)]
        unit_base = top[0]
        q_hg, k_hg, G_hg = cut(1024), cut(1024), cut(1024)
        QK = [cut(1024), cut(1024)]
        E_hg = [xn[:, 0, :], xn[:, 1, :]]
        sg_hg, A_hg, A1_hg, v_hg = cut(1024), cut(1024), cut(512), cut(1024)
        lev_tmp = [cut(512), cut(512)]
        sqT, skT, iqT, sv = cut(512), cut(512), cut(512), cut(512)
        ikT = cut(256)
        iw = cut(16)
        relu = [cut(512), cut(512)]
        score = [cut(256), cut(256)]
        score_left = cut(256)
        sel_bias = [cut(256), cut(256)]
        picks = cut(256)
        m8 = cut(8)
        hpad = cut(2 * 286)
        conv = cut(512)
        conv_d = cut(512)
        diag = cut(1024)
        gate_tmp = lev_tmp
        top[0] = unit_base
        hid = cut(32 * T)
        res_tmp = [cut(512), cut(512)]
        f_sig = [cut(512), cut(512)]
        diag2 = cut(1024)
        top[0] = unit_base
        cT = cut(1024)
        qtok = cut(TT * 768)
        rope_tmp = [cut(256), cut(256)]
        krtok = cut(TT * 96)
        qT_a, kT_a, v_a = cut(2048), cut(2048), cut(1024)
        qT_b, kT_b, v_b = cut(1024), cut(1024), cut(1024)
        sb_e = [cT[:, 0:512], cT[:, 512:1024]]
        sb_suffix = cut(512)
        suffix_mask = cut(512)
        lay = cut(5 * D)
        top[0] = unit_base
        qT_c, kT_c, v_c = cut(2048), cut(2048), cut(2048)
        dT, dtok = cut(256), cut(32)
        f_y, f_l = cut(256), cut(256)

        csil = tiny[:, 0:8]
        mod = tiny[:, 8:56]
        norm_a = tiny[:, 56:64]
        lb = tiny[:, 64:68]
        one_lb = tiny[:, 68:72]
        ssum = tiny[:, 72:80]
        stat = tiny[:, 80:96]
        root = tiny[:, 96:104]
        negmax = tiny[:, 104:110]
        rowsum = tiny[:, 110:116]
        rinv = tiny[:, 116:122]
        need = tiny[:, 122:124]
        count = tiny[:, 124:126]
        lbw = tiny[:, 126:134]
        bn = tiny[:, 136:160]
        mv = tiny[:, 160:168]
        zero8 = tiny[:, 168:176]

        h4 = lambda a: a.rearrange("p (h n) -> p h n", h=4)

        def lay_row(i):
            return lay[:, i * D:(i + 1) * D]

        weights_loaded = [sem(f"weights_loaded{i}") for i in range(SLOTS)]
        weights_started = sem("weights_started")
        psum_full = sem("psum_full")
        bank_read = [sem(f"bank_read{i}") for i in range(BANKS)]
        x_loaded, pcol_loaded, const_loaded = sem("x_loaded"), sem("pcol_loaded"), sem("const_loaded")
        small_loaded, p_loaded, rows_loaded = sem("small_loaded"), sem("p_loaded"), sem("rows_loaded")
        lay_loaded = sem("lay_loaded")
        dve_step, act_step, pool_step = sem("dve_step"), sem("act_step"), sem("pool_step")
        lb_diff_ready, lb_exp_done = sem("lb_diff_ready"), sem("lb_exp_done")
        x_res_ready = sem("x_res_ready")
        c_sig_done, c_ready = sem("c_sig_done"), sem("c_ready")
        squares_summed, root_ready, var_ready = sem("squares_summed"), sem("root_ready"), sem("var_ready")
        xn_ready = sem("xn_ready")
        norm_coef_ready = sem("norm_coef_ready")
        hf_sig_done, f_clipped, logs_done = sem("hf_sig_done"), sem("f_clipped"), sem("logs_done")
        hq_sig_done, hg_sig_done = sem("hq_sig_done"), sem("hg_sig_done")
        conv_done = sem("conv_done")
        conv_sq_ready = sem("conv_sq_ready")
        conv_scaled, conv_sig_done, conv_out_ready = sem("conv_scaled"), sem("conv_sig_done"), sem("conv_out_ready")
        decay_arg_ready, decay_exp_done, qk_ready = sem("decay_arg_ready"), sem("decay_exp_done"), sem("qk_ready")
        levels_summed, o_normed = sem("levels_summed"), sem("o_normed")
        gate_diag_ready = sem("gate_diag_ready")
        relu_used = sem("relu_used")
        logits_ready, exp_done, probs_ready = sem("logits_ready"), sem("exp_done"), sem("probs_ready")
        softplus_done, stick_arg_ready = sem("softplus_done"), sem("stick_arg_ready")
        stick_probs_ready = sem("stick_probs_ready")
        relu2_done = sem("relu2_done")
        silu_sig_done = sem("silu_sig_done")
        q_rope_ready, k_rope_ready = sem("q_rope_ready"), sem("k_rope_ready")
        c_normed = sem("c_normed")
        ple_sig_done = sem("ple_sig_done")
        forget_ln_done, dcum_ready = sem("forget_ln_done"), sem("dcum_ready")
        x_done, out_stored = sem("x_done"), sem("out_stored")

        block = ctx.enter_context(nc.Block())

        @block.sync
        def _(sp):
            n = len(STREAM)
            for i in range(SLOTS):
                sp.dma_start(ring[:, i, :], wstream[i, :, :]).then_inc(weights_loaded[i], 16)
            for i in range(SLOTS, n):
                sp.wait_ge(weights_started, i - SLOTS + 2)
                sp.dma_start(ring[:, i % SLOTS, :], wstream[i, :, :])\
                    .then_inc(weights_loaded[i % SLOTS], 16)
            sp.wait_ge(x_done, 1)
            sp.dma_start(out.rearrange("o (t p) d -> p (o t) d", p=P), x[:, :, :])\
                .then_inc(out_stored, 16)
            sp.wait_ge(out_stored, 16)

        @block.tensor
        def _(pe):
            mm = nc.tensor.matmul
            at = [0]

            def begin(*key):
                assert PLAN[at[0]] == key, (PLAN[at[0]], key)
                at[0] += 1
                u = USE[key]
                if u >= BANKS:
                    pe.wait_ge(bank_read[u % BANKS], u // BANKS)
                return psum[u % BANKS]

            def in_sbuf(*key):
                pe.wait_ge(bank_read[bank(*key)], read(*key))

            def tile(name):
                n = TILE_NO[name]
                pe.wait_ge(weights_loaded[n % SLOTS], 16 * (n // SLOTS + 1))
                return ring[:, n % SLOTS, :], [True]

            def started(ins, first):
                if first[0]:
                    ins.then_inc(weights_started, 1)
                    first[0] = False
                return ins

            def gemm_feature(name, src=hT):
                w, first = tile(name)
                w = w.rearrange("p (k n) -> p k n", k=DC)
                for j in range(2):
                    b = begin(name, j)
                    for o in range(2):
                        for k in range(DC):
                            c = (2 * j + o) * P
                            last = mm(b[:, o * T:(o + 1) * T], w[:, k, c:c + P], src[:, k, :],
                                      start=k == 0, stop=k == DC - 1)
                            started(last, first)
                    last.then_inc(psum_full, 1)

            def gemm_token(name, src=hT):
                w, first = tile(name)
                w = w.rearrange("p (k n) -> p k n", k=DC)
                for t in range(TT):
                    b = begin(name, t)
                    for k in range(DC):
                        last = mm(b[:, :], src[:, k, t * P:(t + 1) * P], w[:, k, :],
                                  start=k == 0, stop=k == DC - 1)
                        started(last, first)
                    last.then_inc(psum_full, 1)

            def to_feature_form(stage, n):
                pe.wait_ge(xn_ready, n)
                for j in range(4):
                    b = begin("tr", stage, j)
                    for c in range(2):
                        for t in range(TT):
                            last = nc.tensor.transpose(
                                b[:, c * T + t * P:c * T + (t + 1) * P],
                                (x if stage == "ple" else xn)[:, t, (2 * j + c) * P:(2 * j + c + 1) * P], ident)
                    last.then_inc(psum_full, 1)
                for j in range(4):
                    in_sbuf("tr", stage, j)

            def modulation(part, tiles):
                b = begin("mod", part)
                for n, i in enumerate(tiles):
                    w, first = tile(f"ada{i}")
                    w = w.rearrange("p (k n) -> p k n", k=DC)
                    for o in range(4):
                        for k in range(DC):
                            last = mm(b[:, 4 * n + o:4 * n + o + 1], w[:, k, o * P:(o + 1) * P],
                                      csil[:, k:k + 1], start=k == 0, stop=k == DC - 1)
                            if not (n == len(tiles) - 1 and o == 3 and k == DC - 1):
                                started(last, first)
                last.then_inc(psum_full, 1)

            def decay_level(lv):
                pe.wait_ge(qk_ready, lv + 1)
                for j in range(1 if lv == 8 else 2):
                    b = begin("lev", lv, j)
                    for i in range(4):
                        if lv == 8:
                            at_ = i * T
                            lhsT, rhs = QK[lv % 2][:, at_:at_ + P], QK[lv % 2][:, at_ + P:at_ + T]
                        else:
                            at_ = (4 * j + i) * P
                            lhsT = rhs = QK[lv % 2][:, at_:at_ + P]
                            if lv == 0:
                                lhsT, rhs = k_hg[:, at_:at_ + P], q_hg[:, at_:at_ + P]
                        last = mm(b[:, i * P:(i + 1) * P], lhsT, rhs, start=True, stop=True)
                    last.then_inc(psum_full, 1)

            def gate_row(i, diag_):
                pe.wait_ge(gate_diag_ready, i + 1)
                for j in range(2):
                    b = begin("grow", i, j)
                    mm(b[:, :], ones[:, 0:P], diag_[:, j * 512:(j + 1) * 512],
                       start=True, stop=True).then_inc(psum_full, 1)

            def attention(name, heads, logits, values, probs, base):
                us = units(heads)
                for key in unit_order(name, len(us)):
                    _, what, i = key
                    g, par, t = us[i]
                    nb = t + 1
                    K = nb * P
                    b = begin(*key)
                    if what == "L":
                        for hh in range(2):
                            last = logits(b[:, hh * K:(hh + 1) * K], 4 * g + par + 2 * hh, t, K)
                    elif what == "T":
                        pe.wait_ge(probs, base + i + 1)
                        p_ = unit_logits[i % 3]
                        for m in range(2 * nb):
                            last = nc.tensor.transpose(b[:, m * P:(m + 1) * P],
                                                       p_[:, m * P:(m + 1) * P], ident)
                    else:
                        in_sbuf(name, "T", i)
                        pT_ = unit_probsT[i % 2]
                        for hh in range(2):
                            for m in range(nb):
                                last = mm(b[par * 64:par * 64 + 64, hh * P:(hh + 1) * P],
                                          values(4 * g + par + 2 * hh, m),
                                          pT_[:, (hh * nb + m) * P:(hh * nb + m + 1) * P],
                                          start=m == 0, stop=m == nb - 1)
                    last.then_inc(psum_full, 1)

            def two_in_rows(qT, kT):
                def logits(o, h, t, K):
                    r = (h % 2) * 64
                    c = (h // 2) * T
                    return mm(o, qT[r:r + 64, c + t * P:c + (t + 1) * P], kT[r:r + 64, c:c + K],
                              start=True, stop=True)
                return logits

            pe.wait_ge(c_ready, 1)
            modulation(0, range(4))
            pe.wait_ge(const_loaded, 16)
            to_feature_form("mix", 1)
            gemm_feature("hf")
            gemm_feature("hq")
            gemm_feature("cu")
            w, first = tile("sviq")
            w = w.rearrange("p (k n) -> p k n", k=DC)
            b = begin("sv")
            for t in range(TT):
                for k in range(DC):
                    last = mm(b[:, t * T:(t + 1) * T], hT[:, k, t * P:(t + 1) * P], w[:, k, 0:T],
                              start=k == 0, stop=k == DC - 1)
                    started(last, first)
            last.then_inc(psum_full, 1)
            b = begin("iq")
            for o in range(2):
                for k in range(DC):
                    last = mm(b[:, o * T:(o + 1) * T], w[:, k, T + o * P:T + (o + 1) * P], hT[:, k, :],
                              start=k == 0, stop=k == DC - 1)
            last.then_inc(psum_full, 1)
            pe.wait_ge(small_loaded, 16)
            wm = small[:, 0:DC * 136].rearrange("p (k n) -> p k n", k=DC)
            b = begin("ik")
            for k in range(DC):
                last = mm(b[:, 0:T], wm[:, k, 0:P], hT[:, k, :], start=k == 0, stop=k == DC - 1)
            last.then_inc(psum_full, 1)
            b = begin("iw")
            for t in range(TT):
                for k in range(DC):
                    last = mm(b[:, t * 8:(t + 1) * 8], hT[:, k, t * P:(t + 1) * P], wm[:, k, P:P + 8],
                              start=k == 0, stop=k == DC - 1)
            last.then_inc(psum_full, 1)
            decay_level(0)
            decay_level(1)
            gemm_feature("sqk")
            decay_level(2)
            decay_level(3)
            gemm_feature("hg")
            decay_level(4)
            decay_level(5)
            gemm_token("hi")
            decay_level(6)
            decay_level(7)
            decay_level(8)
            in_sbuf("iq")
            in_sbuf("ik")
            for t in range(TT):
                K = (t + 1) * P
                for j in range(4):
                    b = begin("sc", t, j)
                    r = 32 * j
                    for hh in range(2):
                        last = mm(b[:, hh * K:(hh + 1) * K],
                                  iqT[r:r + 32, hh * T + t * P:hh * T + (t + 1) * P],
                                  ikT[r:r + 32, 0:K], start=True, stop=True)
                    last.then_inc(psum_full, 1)
            modulation(1, range(4, 12))
            pe.wait_ge(levels_summed, 1)
            in_sbuf("hi", 0)
            in_sbuf("hi", 1)
            in_sbuf("lev", 8, 0)
            b = begin("hgo", 0)
            for h in range(4):
                last = mm(b[:, h * P:(h + 1) * P], A_hg[:, h * T:h * T + P], v_hg[:, h * P:(h + 1) * P],
                          start=True, stop=True)
            last.then_inc(psum_full, 1)
            b = begin("hgo", 1)
            for h in range(4):
                mm(b[:, h * P:(h + 1) * P], A1_hg[:, h * P:(h + 1) * P], v_hg[:, h * P:(h + 1) * P],
                   start=True, stop=False)
                last = mm(b[:, h * P:(h + 1) * P], A_hg[:, h * T + P:(h + 1) * T],
                          v_hg[:, 512 + h * P:512 + (h + 1) * P], start=False, stop=True)
            last.then_inc(psum_full, 1)
            gate_row(0, diag)
            pe.wait_ge(conv_done, 1)
            b = begin("cmean")
            for c in range(2):
                last = mm(b[:, 0:T], avg[:, :], conv[:, c * T:(c + 1) * T], start=c == 0, stop=c == 1)
            last.then_inc(psum_full, 1)
            pe.wait_ge(conv_sq_ready, 1)
            b = begin("cvar")
            for c in range(2):
                last = mm(b[:, 0:T], avg[:, :], conv[:, c * T:(c + 1) * T], start=c == 0, stop=c == 1)
            last.then_inc(psum_full, 1)
            for t in range(TT):
                pe.wait_ge(o_normed, t + 1)
                b = begin("hgt", t)
                for h in range(4):
                    last = nc.tensor.transpose(b[:, h * P:(h + 1) * P],
                                               q_hg[:, t * 512 + h * P:t * 512 + (h + 1) * P], ident)
                last.then_inc(psum_full, 1)
            in_sbuf("sqk", 0)
            in_sbuf("sqk", 1)
            in_sbuf("sv")
            attention("dsa", 4, two_in_rows(sqT, skT),
                      lambda h, m: sv[:, m * T + h * 64:m * T + (h + 1) * 64], probs_ready, 0)
            in_sbuf("hgt", 0)
            in_sbuf("hgt", 1)
            in_sbuf("dsa", "O", 2)
            in_sbuf("dsa", "O", 3)
            pe.wait_ge(conv_out_ready, 1)
            gemm_token("wo0", mixT)
            gemm_token("wo1", mixT)
            to_feature_form("mlp", 2)
            for i in range(8):
                gemm_feature(f"m1_{i}")
            gate_row(1, diag2)
            hid3 = hid.rearrange("p (k n) -> p k n", n=T)

            def down(key, names, chunks, ready):
                banks = {(t, n): begin(*key, t, n) for t in range(TT) for n in range(2)}
                c = 0
                total = sum(chunks)
                for name, m in zip(names, chunks):
                    w, first = tile(name)
                    for i in range(m):
                        ready(c)
                        for t in range(TT):
                            for n in range(2):
                                last = mm(banks[t, n][:, :], hid3[:, c, t * P:(t + 1) * P],
                                          w[:, i * D + n * 512:i * D + (n + 1) * 512],
                                          start=c == 0, stop=c == total - 1)
                                if c == total - 1:
                                    last.then_inc(psum_full, 1)
                                else:
                                    started(last, first)
                        c += 1

            down(("m2",), [f"m2_{i}" for i in range(8)], [4] * 8,
                 lambda c: pe.wait_ge(relu2_done, c // 2 + 1) if c % 2 == 0 else None)
            to_feature_form("fin", 3)
            xn_count = 3
            for layer in range(2):
                if layer == 0:
                    gemm_token("cqkv")
                    wkr = small[:, DC * 152:].rearrange("p (k n) -> p k n", k=DC)
                    b = begin("kr")
                    for t in range(TT):
                        for k in range(DC):
                            last = mm(b[:, t * 32:(t + 1) * 32], hT[:, k, t * P:(t + 1) * P],
                                      wkr[:, k, :], start=k == 0, stop=k == DC - 1)
                    last.then_inc(psum_full, 1)
                    gemm_feature("sbq")
                    gemm_feature("sbk")
                    gemm_token("sbv")
                    for j in range(2):
                        if j == 0:
                            pe.wait_ge(c_normed, 1)
                        b = begin("ct", j)
                        for c in range(2):
                            for t in range(TT):
                                last = nc.tensor.transpose(
                                    b[:, c * T + t * P:c * T + (t + 1) * P],
                                    xn[:, t, (2 * j + c) * P:(2 * j + c + 1) * P], ident)
                        last.then_inc(psum_full, 1)
                    in_sbuf("ct", 0)
                    in_sbuf("ct", 1)
                    cT3 = cT.rearrange("p (k n) -> p k n", n=T)
                    w_lora, first = tile("lora")
                    w_uq = w_lora[:, 0:1536].rearrange("p (k n) -> p k n", k=2)
                    w_ukv = w_lora[:, 1536:3584].rearrange("p (k h e d) -> p k h e d", k=2, h=8, e=2)
                    for t in range(TT):
                        for n in range(2):
                            b = begin("uq", t, n)
                            m = 512 if n == 0 else 256
                            for k in range(2):
                                last = mm(b[:, 0:m], cT3[:, k, t * P:(t + 1) * P],
                                          w_uq[:, k, n * 512:n * 512 + m], start=k == 0, stop=k == 1)
                                started(last, first)
                            last.then_inc(psum_full, 1)
                    for j in range(4):
                        b = begin("uk", j)
                        for o in range(2):
                            for k in range(2):
                                last = mm(b[0:64, o * T:(o + 1) * T], w_ukv[:, k, 2 * j + o, 0, :],
                                          cT3[:, 2 + k, :], start=k == 0, stop=k == 1)
                        last.then_inc(psum_full, 1)
                    for t in range(TT):
                        b = begin("uv", t)
                        for k in range(2):
                            last = mm(b[:, :].rearrange("p (h d) -> p h d", h=8),
                                      cT3[:, 2 + k, t * P:(t + 1) * P], w_ukv[:, k, :, 1, :],
                                      start=k == 0, stop=k == 1)
                        last.then_inc(psum_full, 1)
                    pe.wait_ge(k_rope_ready, 1)
                    b = begin("krt")
                    for t in range(TT):
                        last = nc.tensor.transpose(b[0:96, t * P:(t + 1) * P], krtok[:, t * 96:(t + 1) * 96], ident)
                    last.then_inc(psum_full, 1)
                    for n_ in ("sbq", "sbk", "sbv"):
                        in_sbuf(n_, 0)
                        in_sbuf(n_, 1)
                    attention("sb", 8, two_in_rows(qT_b, kT_b),
                              lambda h, m: v_b[:, m * 512 + h * 64:m * 512 + (h + 1) * 64], stick_probs_ready, 0)
                    pe.wait_ge(q_rope_ready, 1)
                    for j in range(4):
                        b = begin("qt", j)
                        for o in range(2):
                            for t in range(TT):
                                h = 2 * j + o
                                last = nc.tensor.transpose(
                                    b[0:96, o * T + t * P:o * T + (t + 1) * P],
                                    qtok[:, t * 768 + h * 96:t * 768 + (h + 1) * 96], ident)
                        last.then_inc(psum_full, 1)
                    for j in range(4):
                        in_sbuf("qt", j)
                        in_sbuf("uk", j)
                    in_sbuf("krt")
                    in_sbuf("uv", 0)
                    in_sbuf("uv", 1)

                    def mla_logits(o, h, t, K):
                        return mm(o, qT_a[0:96, h * T + t * P:h * T + (t + 1) * P],
                                  kT_a[0:96, h * T:h * T + K], start=True, stop=True)
                    attention("mla", 8, mla_logits,
                              lambda h, m: v_a[:, m * 512 + h * 64:m * 512 + (h + 1) * 64], probs_ready, 4)
                    last_units = [("sb", 8), ("mla", 8)]
                else:
                    b = begin("ff")
                    wf = small[:, DC * 136:DC * 152].rearrange("p (k n) -> p k n", k=DC)
                    for k in range(DC):
                        last = mm(b[0:16, 0:T], wf[:, k, :], hT[:, k, :], start=k == 0, stop=k == DC - 1)
                    last.then_inc(psum_full, 1)
                    for n_ in ["fq0", "fq1", "fk0", "fk1"]:
                        gemm_feature(n_)
                    gemm_token("fv0")
                    gemm_token("fv1")
                    pe.wait_ge(dcum_ready, 1)
                    b = begin("fd")
                    for t in range(TT):
                        last = nc.tensor.transpose(b[:, t * P:(t + 1) * P], dT[:, t * P:(t + 1) * P], ident)
                    last.then_inc(psum_full, 1)
                    for n_ in ["fq0", "fq1", "fk0", "fk1", "fv0", "fv1"]:
                        in_sbuf(n_, 0)
                        in_sbuf(n_, 1)
                    plain = two_in_rows(qT_c, kT_c)
                    negsel = const[:, CONST["negsel"]:CONST["negsel"] + 16]

                    def fox_logits(o, h, t, K):
                        r = (h % 2) * 64
                        c = (h // 2) * T
                        mm(o, negsel[:, h:h + 1].to_broadcast([P, P]), dT[:, 0:K], start=True, stop=False)
                        return mm(o, qT_c[r:r + 64, c + t * P:c + (t + 1) * P], kT_c[r:r + 64, c:c + K],
                                  start=False, stop=True)
                    attention("fox", 16, fox_logits,
                              lambda h, m: v_c[:, m * D + h * 64:m * D + (h + 1) * 64], probs_ready, 12)
                    last_units = [("fox", 16)]
                for n_, m_ in last_units:
                    for i in range(max(0, m_ - BANKS), m_):
                        in_sbuf(n_, "O", i)
                gemm_token(f"o{layer}_0", mixT)
                gemm_token(f"o{layer}_1", mixT)
                xn_count += 1
                to_feature_form(f"ln1_{layer}", xn_count)
                for i in range(11):
                    w, first = tile(f"f13_{layer}_{i}")
                    w = w.rearrange("p (e k n) -> p e k n", e=2, k=DC)
                    for e in range(2):
                        b = begin(f"f13_{layer}_{i}", e)
                        for o in range(2):
                            for k in range(DC):
                                last = mm(b[:, o * T:(o + 1) * T], w[:, e, k, o * P:(o + 1) * P], hT[:, k, :],
                                          start=k == 0, stop=k == DC - 1)
                                started(last, first)
                        last.then_inc(psum_full, 1)
                down(("f2", layer), [f"f2_{layer}_{i}" for i in range(6)], FF2_TILES,
                     lambda c: in_sbuf(f"f13_{layer}_{c // 2}", 1) if c % 2 == 0 else None)
                xn_count += 1
                to_feature_form(f"ln2_{layer}", xn_count)
                if layer == 0:
                    pe.wait_ge(p_loaded, 16)
                w, first = tile(f"pp{layer}")
                w = w[:, 0:2 * D].rearrange("p (k n) -> p k n", k=2)
                for n_ in range(2):
                    for t in range(TT):
                        b = begin("pp", layer, n_, t)
                        for k in range(2):
                            last = mm(b[:, :], pT[:, layer, k, t * P:(t + 1) * P],
                                      w[:, k, n_ * 512:(n_ + 1) * 512], start=k == 0, stop=k == 1)
                            started(last, first)
                        last.then_inc(psum_full, 1)
                for i in range(2):
                    gemm_token(f"pg{layer}_{i}")
                if layer == 0:
                    xn_count += 1
                    to_feature_form("ple", xn_count)

        @block.scalar
        def _(act):
            step = [0]
            A = nc.scalar.activation

            def link(ins):
                step[0] += 1
                ins.then_inc(act_step, 1)
                act.wait_ge(act_step, step[0])

            def wait_full(*key):
                act.wait_ge(psum_full, full(*key))
                return ps(*key)

            def done(ins, *key):
                ins.then_inc(bank_read[bank(*key)], 1)

            def rms_squares(n):
                for t in range(TT):
                    last = A(xn[:, t, :], x[:, t, :], ACT.Square, accum_out=ssum[:, t:t + 1])
                last.then_inc(squares_summed, 1)

            def square_root(width, n):
                act.wait_ge(var_ready, n)
                A(root[:, 0:width], stat[:, 0:width], ACT.Sqrt).then_inc(root_ready, 1)

            def evacuate(stage, scale, shift, wait=None):
                for j in (1, 3):
                    b = wait_full("tr", stage, j)
                    for c in range(2):
                        f = 2 * j + c
                        if scale is None:
                            last = A(hT[:, f, :], b[:, c * T:(c + 1) * T], ACT.Copy)
                        else:
                            last = A(hT[:, f, :], b[:, c * T:(c + 1) * T], ACT.Identity,
                                     scale=scale[:, f:f + 1], bias=shift[:, f:f + 1])
                    done(last, "tr", stage, j)

            def softmax(name, heads, base):
                us = units(heads)
                for i in range(len(us) + 1):
                    if i < len(us):
                        K = (us[i][2] + 1) * P
                        act.wait_ge(logits_ready, base + i + 1)
                        m = 2 * (i % 3)
                        for hh in range(2):
                            L = unit_logits[i % 3][:, hh * K:(hh + 1) * K]
                            last = A(L, L, ACT.Exp, bias=negmax[:, m + hh:m + hh + 1],
                                     accum_out=rowsum[:, m + hh:m + hh + 1])
                        last.then_inc(exp_done, 1)
                    if i >= 1:
                        transposed(name, us, i - 1)

            def transposed(name, us, i):
                K = (us[i][2] + 1) * P
                b = wait_full(name, "T", i)
                if i >= 2:
                    act.wait_ge(psum_full, full(name, "O", i - 2))
                done(A(unit_probsT[i % 2][:, 0:2 * K], b[:, 0:2 * K], ACT.Copy), name, "T", i)

            act.dma_start(pcol[:, :], pcol_in).then_inc(pcol_loaded, 16)
            act.dma_start(x[:, :, :], x_in.rearrange("o (t p) d -> p (o t) d", p=P)).then_inc(x_loaded, 16)
            act.dma_start(const[:, :], const_in).then_inc(const_loaded, 16)
            act.dma_start(small[:, :], wsmall).then_inc(small_loaded, 16)
            act.dma_start(rows[:, 0, :], prow_in[10, :].partition_broadcast(P)).then_inc(rows_loaded, 16)
            act.dma_start(pT[:, :, :, :], p_in.rearrange("p (l k n) -> p l k n", l=2, k=2)).then_inc(p_loaded, 16)
            act.wait_ge(pcol_loaded, 16)
            A(csil, col("c", 0, 8), ACT.Sigmoid).then_inc(c_sig_done, 1)
            act.wait_ge(lb_diff_ready, 1)
            A(lbw[:, 0:4], lbw[:, 0:4], ACT.Exp).then_inc(lb_exp_done, 1)
            act.wait_ge(x_loaded, 16)
            rms_squares(1)
            square_root(TT, 1)
            act.wait_ge(norm_coef_ready, 1)
            evacuate("mix", norm_a, mod[:, 0:8])
            for j in range(2):
                b = wait_full("hf", j)
                A(G_hg[:, j * 512:(j + 1) * 512], b[:, :], ACT.Sigmoid)
                last = A(k_hg[:, j * 512:(j + 1) * 512], b[:, :], ACT.Sigmoid, scale=-1.0)
                done(last, "hf", j)
            for j in range(2):
                b = wait_full("hq", j)
                A(q_hg[:, j * 512:(j + 1) * 512], b[:, :], ACT.Sigmoid).then_inc(hq_sig_done, 1)
            act.wait_ge(f_clipped, 1)
            A(G_hg, G_hg, ACT.Ln)
            A(QK[0], QK[0], ACT.Ln).then_inc(logs_done, 1)
            b = wait_full("cu", 1)
            done(A(conv_d, b[:, :], ACT.Sigmoid), "cu", 1)
            b = wait_full("sv")
            done(A(sv, b[:, :], ACT.Copy), "sv")
            b = wait_full("iq")
            done(A(iqT, b[:, :], ACT.Copy), "iq")
            b = wait_full("ik")
            done(A(ikT, b[:, 0:T], ACT.Copy), "ik")
            b = wait_full("iw")
            done(A(iw, b[:, 0:16], ACT.Copy), "iw")

            def decay_exp(lv):
                act.wait_ge(decay_arg_ready, lv)
                A(E_hg[lv % 2], E_hg[lv % 2], ACT.Exp).then_inc(decay_exp_done, 1)

            decay_exp(1)
            decay_exp(2)
            for j in range(2):
                b = wait_full("sqk", j)
                done(A((sqT, skT)[j], b[:, :], ACT.Copy), "sqk", j)
            decay_exp(3)
            decay_exp(4)
            for j in range(2):
                b = wait_full("hg", j)
                A(sg_hg[:, j * 512:(j + 1) * 512], b[:, :], ACT.Sigmoid).then_inc(hg_sig_done, 1)
            decay_exp(5)
            decay_exp(6)
            for t in range(TT):
                b = wait_full("hi", t)
                done(A(v_hg[:, t * 512:(t + 1) * 512], b[:, :], ACT.Copy), "hi", t)
            decay_exp(7)
            decay_exp(8)
            b = wait_full("lev", 8, 0)
            done(A(A1_hg, b[:, :], ACT.Copy), "lev", 8, 0)
            for t in range(TT):
                K = (t + 1) * P
                for j in range(4):
                    i = 4 * t + j
                    b = wait_full("sc", t, j)
                    if i >= 2:
                        act.wait_ge(relu_used, i - 1)
                    done(A(relu[i % 2][:, 0:2 * K], b[:, 0:2 * K], ACT.Relu, scale=1.0 / 16), "sc", t, j)
            for t in range(TT):
                b = wait_full("hgo", t)
                o = k_hg[:, t * 512:(t + 1) * 512]
                A(o, b[:, :], ACT.Copy)
                for h in range(4):
                    last = A(G_hg[:, (4 * t + h) * P:(4 * t + h + 1) * P], b[:, h * P:(h + 1) * P], ACT.Square,
                             accum_out=ssum[:, 4 * t + h:4 * t + h + 1])
                done(last, "hgo", t)
            square_root(8, 2)
            act.wait_ge(bank_read[bank("cvar")], read("cvar"))
            A(hpad[:, 0:T], hpad[:, 0:T], ACT.Sqrt).then_inc(root_ready, 1)
            act.wait_ge(conv_scaled, 1)
            for c in range(2):
                last = A(conv_d[:, c * T:(c + 1) * T], conv[:, c * T:(c + 1) * T], ACT.Sigmoid)
            last.then_inc(conv_sig_done, 1)
            softmax("dsa", 4, 0)
            act.wait_ge(x_res_ready, 1)
            rms_squares(2)
            square_root(TT, 4 - 1)
            evacuate("mlp", norm_a, mod[:, 24:32])
            for i in range(8):
                for j in range(2):
                    b = wait_full(f"m1_{i}", j)
                    done(A(hid[:, (4 * i + 2 * j) * T:(4 * i + 2 * j + 2) * T], b[:, :], ACT.Relu), f"m1_{i}", j)
            act.wait_ge(x_res_ready, 2)
            rms_squares(3)
            square_root(TT, 4)
            evacuate("fin", col("fin_w", 0, 8), zero8)
            act.wait_ge(psum_full, full("tr", "fin", 3))
            act.dma_start(lay.rearrange("p (r n) -> p r n", r=5),
                          prow_in[0:5, :].partition_broadcast(P)).then_inc(lay_loaded, 16)
            roots = 4
            base = 4
            for layer in range(2):
                if layer == 0:
                    for t in range(TT):
                        b = wait_full("cqkv", t)
                        A(xn[:, t, 0:512], b[:, :], ACT.Copy)
                        for e in range(2):
                            last = A(xn[:, t, 512 + e * T:512 + (e + 1) * T], b[:, e * T:(e + 1) * T], ACT.Square,
                                     accum_out=ssum[:, 2 * t + e:2 * t + e + 1])
                        done(last, "cqkv", t)
                    roots += 1
                    square_root(4, roots)
                    for j in range(2):
                        b = wait_full("sbq", j)
                        done(A(qT_b[:, j * 512:(j + 1) * 512], b[:, :], ACT.Copy, scale=0.125), "sbq", j)
                    for j in range(2):
                        b = wait_full("sbk", j)
                        done(A(kT_b[:, j * 512:(j + 1) * 512], b[:, :], ACT.Copy), "sbk", j)
                    for j in range(2):
                        b = wait_full("sbv", j)
                        done(A(v_b[:, j * 512:(j + 1) * 512], b[:, :], ACT.Copy), "sbv", j)
                    for j in range(2):
                        b = wait_full("ct", j)
                        for c in range(2):
                            g = col("q_norm" if j == 0 else "kv_norm", c)
                            last = A(cT[:, (2 * j + c) * T:(2 * j + c + 1) * T], b[:, c * T:(c + 1) * T],
                                     ACT.Copy, scale=g)
                        done(last, "ct", j)
                    for t in range(TT):
                        for n in range(2):
                            m = 512 if n == 0 else 256
                            b = wait_full("uq", t, n)
                            done(A(qtok[:, t * 768 + n * 512:t * 768 + n * 512 + m], b[:, 0:m], ACT.Copy), "uq", t, n)
                    for j in range(4):
                        b = wait_full("uk", j)
                        done(A(kT_a[0:64, j * 512:(j + 1) * 512], b[0:64, :], ACT.Copy), "uk", j)
                    for t in range(TT):
                        b = wait_full("uv", t)
                        done(A(v_a[:, t * 512:(t + 1) * 512], b[:, :], ACT.Copy), "uv", t)
                    us = units(8)
                    for i in range(len(us) + 1):
                        if i < len(us):
                            K = (us[i][2] + 1) * P
                            e = sb_e[i % 2][:, 0:2 * K]
                            act.wait_ge(bank_read[bank("sb", "L", i)], read("sb", "L", i))
                            link(A(e, unit_logits[i % 3][:, 0:2 * K], ACT.Abs))
                            link(A(e, e, ACT.Exp, scale=-1.0))
                            A(e, e, ACT.Ln, bias=1.0).then_inc(softplus_done, 1)
                        if i >= 1:
                            K = (us[i - 1][2] + 1) * P
                            act.wait_ge(stick_arg_ready, i)
                            L = unit_logits[(i - 1) % 3][:, 0:2 * K]
                            A(L, L, ACT.Exp).then_inc(stick_probs_ready, 1)
                            transposed("sb", us, i - 1)
                    for j in range(4):
                        b = wait_full("qt", j)
                        done(A(qT_a[0:96, j * 512:(j + 1) * 512], b[0:96, :], ACT.Copy), "qt", j)
                    softmax("mla", 8, base)
                    base += 8
                else:
                    act.wait_ge(bank_read[bank("ff")], read("ff"))
                    link(A(f_l[0:16, :], f_y[0:16, :], ACT.Abs))
                    link(A(f_l[0:16, :], f_l[0:16, :], ACT.Exp, scale=-1.0))
                    A(f_l[0:16, :], f_l[0:16, :], ACT.Ln, bias=1.0).then_inc(forget_ln_done, 1)
                    for n_, dst, s in [("fq0", qT_c[:, 0:1024], 0.125), ("fq1", qT_c[:, 1024:2048], 0.125),
                                       ("fk0", kT_c[:, 0:1024], 1.0), ("fk1", kT_c[:, 1024:2048], 1.0)]:
                        for j in range(2):
                            b = wait_full(n_, j)
                            done(A(dst[:, j * 512:(j + 1) * 512], b[:, :], ACT.Copy, scale=s), n_, j)
                    for n in range(2):
                        for t in range(TT):
                            b = wait_full(f"fv{n}", t)
                            done(A(v_c[:, t * D + n * 512:t * D + (n + 1) * 512], b[:, :], ACT.Copy), f"fv{n}", t)
                    softmax("fox", 16, base)
                    base += 16
                roots += 1
                square_root(TT, roots)
                evacuate(f"ln1_{layer}", col(f"ln1_g{layer}", 0, 8), col(f"ln1_b{layer}", 0, 8))
                for i in range(11):
                    b = wait_full(f"f13_{layer}_{i}", 0)
                    if i >= 2:
                        act.wait_ge(bank_read[bank(f"f13_{layer}_{i - 2}", 1)], read(f"f13_{layer}_{i - 2}", 1))
                    A(f_sig[i % 2], b[:, :], ACT.Sigmoid).then_inc(silu_sig_done, 1)
                roots += 1
                square_root(TT, roots)
                evacuate(f"ln2_{layer}", col(f"ln2_g{layer}", 0, 8), col(f"ln2_b{layer}", 0, 8))
                for i in range(4):
                    key = (f"pg{layer}_{i // 2}", i % 2)
                    act.wait_ge(bank_read[bank(*key)], read(*key))
                    z = xn[:, i // 2, (i % 2) * 512:(i % 2 + 1) * 512]
                    A(z, z, ACT.Sigmoid).then_inc(ple_sig_done, 1)
                if layer == 0:
                    evacuate("ple", None, None)
                    act.dma_start(lay.rearrange("p (r n) -> p r n", r=5),
                                  prow_in[5:10, :].partition_broadcast(P)).then_inc(lay_loaded, 16)

        @block.gpsimd
        def _(pool):
            step = [0]

            def link(ins):
                step[0] += 1
                ins.then_inc(pool_step, 1)
                pool.wait_ge(pool_step, step[0])

            pool.wait_ge(pcol_loaded, 16)
            pool.wait_ge(bank_read[bank("cu", 0)], read("cu", 0))
            hp = hpad.rearrange("p (c n) -> p c n", c=2)
            acc = conv.rearrange("p (c n) -> p c n", c=2)
            for j in range(31):
                product = mixT[:, 4 + 2 * (j % 2):6 + 2 * (j % 2), :]
                w = col("cv_w", 2 * j, 2).unsqueeze(2).to_broadcast([P, 2, T])
                link(nc.gpsimd.tensor_tensor(product, hp[:, :, j:j + T], w, ALU.mult))
                before = col("cv_b", 0, 2).unsqueeze(2).to_broadcast([P, 2, T]) if j == 0 else acc
                last = nc.gpsimd.tensor_tensor(acc, product, before, ALU.add)
            last.then_inc(conv_done, 1)
            for i in range(8):
                for j in range(2):
                    pool.wait_ge(bank_read[bank(f"m1_{i}", j)], read(f"m1_{i}", j))
                    r = hid[:, (4 * i + 2 * j) * T:(4 * i + 2 * j + 2) * T]
                    nc.gpsimd.tensor_tensor(r, r, r, ALU.mult).then_inc(relu2_done, 1)

        @block.vector
        def _(dve):
            step = [0]
            V = nc.vector

            def link(ins):
                step[0] += 1
                ins.then_inc(dve_step, 1)
                dve.wait_ge(dve_step, step[0])

            def wait_full(*key):
                dve.wait_ge(psum_full, full(*key))
                return ps(*key)

            def done(ins, *key):
                ins.then_inc(bank_read[bank(*key)], 1)
                dve.wait_ge(bank_read[bank(*key)], read(*key))

            made = {}

            def own(s):
                made[s.name] = made.get(s.name, 0) + 1
                dve.wait_ge(s, made[s.name])

            def wait_done(*key):
                dve.wait_ge(bank_read[bank(*key)], read(*key))

            def evacuate(stage, scale, shift):
                for j in (0, 2):
                    b = wait_full("tr", stage, j)
                    for c in range(2):
                        f = 2 * j + c
                        if scale is None:
                            last = V.tensor_copy(hT[:, f, :], b[:, c * T:(c + 1) * T])
                        else:
                            last = V.tensor_scalar(hT[:, f, :], b[:, c * T:(c + 1) * T],
                                                   scale[:, f:f + 1], shift[:, f:f + 1], ALU.mult, ALU.add)
                    done(last, "tr", stage, j)

            roots = [0]

            def rstd(width, scale, eps, src):
                V.tensor_scalar(stat[:, 0:width], src, scale, eps, ALU.mult, ALU.add).then_inc(var_ready, 1)
                own(var_ready)
                roots[0] += 1
                dve.wait_ge(root_ready, roots[0] + extra_roots[0])
                link(V.reciprocal(stat[:, 8:8 + width], root[:, 0:width]))

            extra_roots = [0]

            def rms_norm(n):
                dve.wait_ge(squares_summed, n)
                rstd(TT, 1.0 / D, EPS, ssum[:, 0:TT])
                for t in range(TT):
                    last = V.tensor_scalar(xn[:, t, :], x[:, t, :], stat[:, 8 + t:9 + t], None, ALU.mult)
                last.then_inc(xn_ready, 1)
                own(xn_ready)

            def softmax(name, heads, base, bias, scale, c0):
                us = units(heads)
                n = len(us)
                for i in range(n + 2):
                    if i < n:
                        g, par, t = us[i]
                        K = (t + 1) * P
                        m = 2 * (i % 3)
                        b = wait_full(name, "L", i)
                        L = unit_logits[i % 3][:, 0:2 * K].rearrange("p (h k) -> p h k", h=2)
                        if name == "fox":
                            for hh in range(2):
                                h = 4 * g + par + 2 * hh
                                last = V.scalar_tensor_tensor(out=L[:, hh, :], in0=b[:, hh * K:(hh + 1) * K],
                                                              scalar=dtok[:, t * 16 + h:t * 16 + h + 1],
                                                              in1=bias(t), op0=ALU.add, op1=ALU.add)
                        else:
                            last = V.scalar_tensor_tensor(
                                out=L, in0=b[:, 0:2 * K].rearrange("p (h k) -> p h k", h=2), scalar=scale,
                                in1=bias(t).unsqueeze(1).to_broadcast([P, 2, K]), op0=ALU.mult, op1=ALU.add)
                        done(last, name, "L", i)
                        wait_done(name, "L", i)
                        V.tensor_reduce(negmax[:, m:m + 2], L, AX.X, ALU.max, negate=True).then_inc(logits_ready, 1)
                        own(logits_ready)
                    if 0 <= i - 1 < n:
                        t = us[i - 1][2]
                        K = (t + 1) * P
                        m = 2 * ((i - 1) % 3)
                        dve.wait_ge(exp_done, base_exp[0] + i)
                        link(V.reciprocal(rinv[:, m:m + 2], rowsum[:, m:m + 2]))
                        for hh in range(2):
                            L = unit_logits[(i - 1) % 3][:, hh * K:(hh + 1) * K]
                            last = V.tensor_scalar(L, L, rinv[:, m + hh:m + hh + 1], None, ALU.mult)
                        last.then_inc(probs_ready, 1)
                        own(probs_ready)
                    if 0 <= i - 2 < n:
                        unit_output(name, us, i - 2, c0)
                base_exp[0] += n

            base_exp = [0]

            def unit_output(name, us, i, c0):
                g, par, t = us[i]
                b = wait_full(name, "O", i)
                r = par * 64
                done(V.tensor_copy(mixT[r:r + 64, c0 + 2 * g:c0 + 2 * g + 2, t * P:(t + 1) * P],
                                   b[r:r + 64, 0:T].rearrange("p (c n) -> p c n", c=2)), name, "O", i)

            V.memset(avg[:, :], 1.0 / 256)
            V.memset(zero8, 0.0)
            V.memset(hpad, 0.0)
            link(V.memset(ones[:, :], 1.0))
            dve.wait_ge(pcol_loaded, 16)
            V.tensor_tensor(lbw[:, 0:4], col("lb", 0, 4), col("lb", 0, 4), ALU.subtract).then_inc(lb_diff_ready, 1)
            own(lb_diff_ready)
            dve.wait_ge(lb_exp_done, 1)
            link(V.reciprocal(lbw[:, 4:8], lbw[:, 0:4]))
            link(V.tensor_tensor(lbw[:, 0:4], lbw[:, 0:4], lbw[:, 4:8], ALU.mult))
            link(V.tensor_tensor(lb, lbw[:, 0:4], lbw[:, 0:4], ALU.subtract))
            V.tensor_scalar(one_lb, lb, -1.0, 1.0, ALU.mult, ALU.add)
            dve.wait_ge(c_sig_done, 1)
            V.tensor_tensor(csil, csil, col("c", 0, 8), ALU.mult).then_inc(c_ready, 1)
            own(c_ready)
            rms_norm(1)
            b = wait_full("mod", 0)
            done(V.tensor_tensor(mod[:, 0:16], b[:, 0:16], col("ada_b", 0, 16), ALU.add), "mod", 0)
            wait_done("mod", 0)
            V.scalar_tensor_tensor(out=norm_a, in0=mod[:, 8:16], scalar=1.0, in1=col("mix_w", 0, 8),
                                   op0=ALU.add, op1=ALU.mult).then_inc(norm_coef_ready, 1)
            own(norm_coef_ready)
            evacuate("mix", norm_a, mod[:, 0:8])
            for j in range(2):
                wait_done("hf", j)
            for h in range(4):
                s = slice(h * T, (h + 1) * T)
                V.tensor_scalar(k_hg[:, s], k_hg[:, s], one_lb[:, h:h + 1], None, ALU.mult)
                last = V.tensor_scalar(G_hg[:, s], G_hg[:, s], one_lb[:, h:h + 1], lb[:, h:h + 1], ALU.mult, ALU.add)
            link(last)
            link(V.tensor_scalar(G_hg, G_hg, TINY, None, ALU.max))
            link(V.tensor_scalar(QK[0], G_hg, LN_SPLIT, 1.0, ALU.mult, ALU.min))
            V.tensor_scalar(G_hg, G_hg, 1.0 / LN_SPLIT, None, ALU.max).then_inc(f_clipped, 1)
            own(f_clipped)
            for j in range(2):
                b = wait_full("hq", j)
                dve.wait_ge(hq_sig_done, j + 1)
                s = slice(j * 512, (j + 1) * 512)
                done(V.scalar_tensor_tensor(out=q_hg[:, s], in0=b[:, :], scalar=P ** -0.5, in1=q_hg[:, s],
                                            op0=ALU.mult, op1=ALU.mult), "hq", j)
            dve.wait_ge(logs_done, 1)
            link(V.tensor_tensor(G_hg, G_hg, QK[0], ALU.add))
            for h in range(4):
                s = slice(h * T, (h + 1) * T)
                last = V.tensor_tensor_scan(E_hg[0][:, s], ones[:, :], G_hg[:, s], 0.0, ALU.mult, ALU.add)
            link(last)
            V.tensor_copy(G_hg, E_hg[0]).then_inc(qk_ready, 1)
            own(qk_ready)

            def halves(a, bsz):
                v = a.rearrange("p (n two b) -> p n two b", two=2, b=bsz)
                return v[:, :, 0, :], v[:, :, 1, :]

            def decay_args(lv):
                bsz = 1 << (lv - 1)
                left, right = halves(G_hg, bsz)
                el, er = halves(E_hg[lv % 2], bsz)
                n = 512 // bsz
                ref = left[:, :, bsz - 1:bsz].to_broadcast([P, n, bsz])
                V.tensor_tensor(el, ref, left, ALU.subtract)
                V.tensor_tensor(er, right, ref, ALU.subtract).then_inc(decay_arg_ready, 1)
                own(decay_arg_ready)

            def decay_factors(lv):
                bsz = 1 << (lv - 1)
                dve.wait_ge(decay_exp_done, lv)
                kl, _ = halves(k_hg, bsz)
                _, qr = halves(q_hg, bsz)
                el, er = halves(E_hg[lv % 2], bsz)
                ol, orr = halves(QK[lv % 2], bsz)
                if lv >= 3:
                    dve.wait_ge(psum_full, full("lev", lv - 2, 1))
                V.tensor_tensor(ol, kl, el, ALU.mult)
                V.tensor_tensor(orr, qr, er, ALU.mult).then_inc(qk_ready, 1)
                own(qk_ready)

            def decay_sum(lv):
                at = CONST["levels"] + (lv - 1) * P
                m = (ident if lv == 0 else const[:, at:at + P]).unsqueeze(1).to_broadcast([P, 4, P])
                for j in range(2):
                    b = wait_full("lev", lv, j)
                    Aj = A_hg[:, j * 512:(j + 1) * 512]
                    dst = Aj if lv == 0 else lev_tmp[j]
                    done(V.tensor_tensor(h4(dst), h4(b[:, :]), m, ALU.mult), "lev", lv, j)
                if lv:
                    for j in range(2):
                        wait_done("lev", lv, j)
                        Aj = A_hg[:, j * 512:(j + 1) * 512]
                        last = V.tensor_tensor(Aj, Aj, lev_tmp[j], ALU.add)
                    if lv == 7:
                        last.then_inc(levels_summed, 1)
                        own(levels_summed)
                    else:
                        link(last)
                else:
                    for j in range(2):
                        wait_done("lev", lv, j)

            decay_args(1)
            decay_args(2)
            wait_done("cu", 1)
            b = wait_full("cu", 0)
            done(V.tensor_tensor(hpad.rearrange("p (c n) -> p c n", c=2)[:, :, 30:286],
                                 b[:, :].rearrange("p (c n) -> p c n", c=2),
                                 conv_d.rearrange("p (c n) -> p c n", c=2), ALU.mult), "cu", 0)
            decay_factors(1)
            for lv in range(2, 9):
                if lv + 1 <= 8:
                    decay_args(lv + 1)
                decay_factors(lv)
                decay_sum(lv - 2)
                if lv == 5:
                    for j in range(2):
                        b = wait_full("hg", j)
                        dve.wait_ge(hg_sig_done, j + 1)
                        for c in range(2):
                            h = 2 * j + c
                            s = slice(h * T, (h + 1) * T)
                            last = V.scalar_tensor_tensor(out=sg_hg[:, s], in0=b[:, c * T:(c + 1) * T],
                                                          scalar=col("onorm", h), in1=sg_hg[:, s],
                                                          op0=ALU.mult, op1=ALU.mult)
                        done(last, "hg", j)
            decay_sum(7)
            wait_done("iw")
            for t in range(TT):
                K = (t + 1) * P
                sc, B = score[t][:, 0:K], bias_of("causal", t)
                for j in range(4):
                    wait_done("sc", t, j)
                    r = relu[(4 * t + j) % 2]
                    for hh in range(2):
                        ins = V.scalar_tensor_tensor(
                            out=sc, in0=r[:, hh * K:(hh + 1) * K], scalar=iw[:, t * 8 + j + 4 * hh:t * 8 + j + 4 * hh + 1],
                            in1=B if j + hh == 0 else sc, op0=ALU.mult, op1=ALU.add)
                        if hh == 1:
                            ins.then_inc(relu_used, 1)
                            own(relu_used)
                        else:
                            link(ins)
                left = score_left[:, 0:K]
                cur = sc
                for r_ in range(TOPK // 8):
                    link(V.max(m8, cur))
                    if r_ < TOPK // 8 - 1:
                        link(V.match_replace(left, m8, cur, -3.0e38))
                        cur = left
                thr = m8[:, 7:8]
                pk = picks[:, 0:K]
                link(V.tensor_scalar(pk, sc, thr, 0.0, ALU.is_gt, ALU.add, accum_out=count[:, 0:1]))
                link(V.tensor_scalar(need[:, 0:1], count[:, 0:1], -1.0, float(TOPK), ALU.mult, ALU.add))
                link(V.tensor_scalar(sc, sc, thr, None, ALU.is_equal))
                link(V.tensor_tensor_scan(left, ones[:, 0:K], sc, 0.0, ALU.mult, ALU.add))
                link(V.scalar_tensor_tensor(out=left, in0=left, scalar=need[:, 0:1], in1=sc,
                                            op0=ALU.is_le, op1=ALU.mult))
                link(V.tensor_tensor(pk, pk, left, ALU.add))
                link(V.tensor_scalar(pk, pk, -1.0, -NEG, ALU.add, ALU.mult))
                link(V.tensor_tensor(sel_bias[t][:, 0:K], pk, B, ALU.add))
            b = wait_full("mod", 1)
            done(V.tensor_tensor(mod[:, 16:48], b[:, 0:32], col("ada_b", 16, 32), ALU.add), "mod", 1)
            wait_done("mod", 1)
            V.tensor_tensor(diag.rearrange("p (c n) -> p c n", c=DC), ident.unsqueeze(1).to_broadcast([P, DC, P]),
                            mod[:, 16:24].unsqueeze(2).to_broadcast([P, DC, P]), ALU.mult).then_inc(gate_diag_ready, 1)
            own(gate_diag_ready)
            V.scalar_tensor_tensor(out=norm_a, in0=mod[:, 32:40], scalar=1.0, in1=col("mlp_w", 0, 8),
                                   op0=ALU.add, op1=ALU.mult)
            wait_done("hgo", 0)
            wait_done("hgo", 1)
            rstd(8, 1.0 / P, EPS, ssum[:, 0:8])
            for t in range(TT):
                V.tensor_tensor(h4(q_hg[:, t * 512:(t + 1) * 512]), h4(k_hg[:, t * 512:(t + 1) * 512]),
                                stat[:, 8 + 4 * t:12 + 4 * t].unsqueeze(2).to_broadcast([P, 4, P]),
                                ALU.mult).then_inc(o_normed, 1)
                own(o_normed)
            for j in range(2):
                b = wait_full("grow", 0, j)
                done(V.tensor_copy(rows[:, 1, j * 512:(j + 1) * 512], b[:, :]), "grow", 0, j)
            c2 = lambda a: a.rearrange("p (c n) -> p c n", c=2)
            b = wait_full("cmean")
            done(V.tensor_tensor(c2(conv_d), c2(conv), b[:, 0:T].unsqueeze(1).to_broadcast([P, 2, T]),
                                 ALU.subtract), "cmean")
            wait_done("cmean")
            V.tensor_tensor(conv, conv_d, conv_d, ALU.mult).then_inc(conv_sq_ready, 1)
            own(conv_sq_ready)
            b = wait_full("cvar")
            done(V.tensor_scalar(hpad[:, 0:T], b[:, 0:T], EPS, None, ALU.add), "cvar")
            wait_done("cvar")
            extra_roots[0] += 1
            dve.wait_ge(root_ready, roots[0] + extra_roots[0])
            link(V.reciprocal(hpad[:, T:2 * T], hpad[:, 0:T]))
            link(V.tensor_tensor(c2(conv_d), c2(conv_d), hpad[:, T:2 * T].unsqueeze(1).to_broadcast([P, 2, T]),
                                 ALU.mult))
            for c in range(2):
                s = slice(c * T, (c + 1) * T)
                last = V.tensor_scalar(conv[:, s], conv_d[:, s], col("cv_ln_w", c), col("cv_ln_b", c),
                                       ALU.mult, ALU.add)
            last.then_inc(conv_scaled, 1)
            own(conv_scaled)
            dve.wait_ge(conv_sig_done, 1)
            V.tensor_tensor(mixT[:, 6:8, :], c2(conv), c2(conv_d), ALU.mult).then_inc(conv_out_ready, 1)
            own(conv_out_ready)
            for t in range(TT):
                b = wait_full("hgt", t)
                done(V.tensor_tensor(mixT[:, 0:4, t * P:(t + 1) * P], h4(b[:, :]),
                                     sg_hg.rearrange("p (h n) -> p h n", h=4)[:, :, t * P:(t + 1) * P],
                                     ALU.mult), "hgt", t)
            softmax("dsa", 4, 0, lambda t: sel_bias[t][:, 0:(t + 1) * P], 0.125, 4)

            def gated_residual(keys):
                for i, (key, t, n) in enumerate(keys):
                    b = wait_full(*key)
                    done(V.tensor_tensor(gate_tmp[i % 2], b[:, :], rows[:, 1, n * 512:(n + 1) * 512], ALU.mult), *key)
                    wait_done(*key)
                    xs = x[:, t, n * 512:(n + 1) * 512]
                    last = V.tensor_tensor(xs, xs, gate_tmp[i % 2], ALU.add)
                last.then_inc(x_res_ready, 1)
                own(x_res_ready)

            gated_residual([((f"wo{n}", t), t, n) for n in range(2) for t in range(TT)])
            rms_norm(2)
            evacuate("mlp", norm_a, mod[:, 24:32])
            V.tensor_tensor(diag2.rearrange("p (c n) -> p c n", c=DC), ident.unsqueeze(1).to_broadcast([P, DC, P]),
                            mod[:, 40:48].unsqueeze(2).to_broadcast([P, DC, P]), ALU.mult).then_inc(gate_diag_ready, 1)
            own(gate_diag_ready)
            for j in range(2):
                b = wait_full("grow", 1, j)
                done(V.tensor_copy(rows[:, 1, j * 512:(j + 1) * 512], b[:, :]), "grow", 1, j)
                wait_done("grow", 1, j)

            def gated_residual2():
                for i, (t, n) in enumerate([(t, n) for t in range(TT) for n in range(2)]):
                    b = wait_full("m2", t, n)
                    done(V.tensor_tensor(res_tmp[i % 2], b[:, :], rows[:, 1, n * 512:(n + 1) * 512], ALU.mult),
                         "m2", t, n)
                    wait_done("m2", t, n)
                    xs = x[:, t, n * 512:(n + 1) * 512]
                    last = V.tensor_tensor(xs, xs, res_tmp[i % 2], ALU.add)
                last.then_inc(x_res_ready, 1)
                own(x_res_ready)

            gated_residual2()
            rms_norm(3)
            dve.wait_ge(rows_loaded, 16)
            for t in range(TT):
                last = V.tensor_tensor(x[:, t, :], xn[:, t, :], rows[:, 0, :], ALU.mult)
            link(last)
            evacuate("fin", col("fin_w", 0, 8), zero8)
            xn_made = 3
            base_exp[0] = 4

            def layer_norm(keys, g_row, b_row, stage, layer):
                for i, (key, t, n) in enumerate(keys):
                    b = wait_full(*key)
                    xs = x[:, t, n * 512:(n + 1) * 512]
                    done(V.scalar_tensor_tensor(out=xs, in0=xs, scalar=ALPHA, in1=b[:, :], op0=ALU.mult, op1=ALU.add),
                         *key)
                    wait_done(*key)
                    last = V.bn_stats(bn[:, (2 * t + n) * 6:(2 * t + n + 1) * 6], xs)
                link(last)
                for t in range(TT):
                    last = V.bn_aggr(mv[:, 2 * t:2 * t + 2], bn[:, 12 * t:12 * t + 12].rearrange("p (a b) -> p a b", a=2))
                link(last)
                rstd(TT, 1.0, EPS_LN, mv[:, 0:4].rearrange("p (t e) -> p t e", e=2)[:, :, 1])
                for t in range(TT):
                    last = V.tensor_scalar(xn[:, t, :], x[:, t, :], mv[:, 2 * t:2 * t + 1], stat[:, 8 + t:9 + t],
                                           ALU.subtract, ALU.mult)
                last.then_inc(xn_ready, 1)
                own(xn_ready)
                if layer == 0 and g_row == 0:
                    dve.wait_ge(lay_loaded, 16)
                if layer == 1 and g_row == 0:
                    dve.wait_ge(lay_loaded, 32)
                evacuate(stage, col(f"ln{1 + g_row // 2}_g{layer}", 0, 8), col(f"ln{1 + g_row // 2}_b{layer}", 0, 8))
                for t in range(TT):
                    last = V.tensor_tensor(x[:, t, :], xn[:, t, :], lay_row(g_row), ALU.mult)
                link(last)
                for t in range(TT):
                    last = V.tensor_tensor(x[:, t, :], x[:, t, :], lay_row(b_row), ALU.add)
                link(last)

            for layer in range(2):
                if layer == 0:
                    wait_done("cqkv", 0)
                    wait_done("cqkv", 1)
                    rstd(4, 1.0 / 256, EPS, ssum[:, 0:4])
                    for t in range(TT):
                        for e in range(2):
                            s = xn[:, t, e * T:(e + 1) * T]
                            last = V.tensor_scalar(s, s, stat[:, 8 + 2 * t + e:9 + 2 * t + e], None, ALU.mult)
                    last.then_inc(c_normed, 1)
                    own(c_normed)
                    link(V.memset(krtok, 0.0))
                    V.memset(suffix_mask, 1.0)
                    b = wait_full("kr")
                    kraw = rope_tmp[0][:, 0:64]
                    done(V.tensor_copy(kraw, b[:, 0:64]), "kr")
                    wait_done("kr")
                    V.memset(suffix_mask[:, 255:256], 0.0)

                    def rope(x1, x2, o1, o2, cos, sin, t1, t2, t3, t4):
                        V.tensor_tensor(t1, x1, cos, ALU.mult)
                        V.tensor_tensor(t2, x2, sin, ALU.mult)
                        V.tensor_tensor(t3, x1, sin, ALU.mult)
                        link(V.tensor_tensor(t4, x2, cos, ALU.mult))
                        V.tensor_tensor(o1, t1, t2, ALU.subtract)
                        return V.tensor_tensor(o2, t3, t4, ALU.add)

                    cosv = const[:, CONST["cos"]:CONST["cos"] + 32].rearrange("p (t d) -> p t d", t=2)
                    sinv = const[:, CONST["sin"]:CONST["sin"] + 32].rearrange("p (t d) -> p t d", t=2)
                    kv3 = kraw.rearrange("p (t d) -> p t d", t=2)
                    kt3 = krtok.rearrange("p (t d) -> p t d", t=2)
                    tm = [rope_tmp[1][:, 32 * i:32 * i + 32].rearrange("p (t d) -> p t d", t=2) for i in range(4)]
                    rope(kv3[:, :, 0:16], kv3[:, :, 16:32], kt3[:, :, 64:80], kt3[:, :, 80:96], cosv, sinv, *tm)\
                        .then_inc(k_rope_ready, 1)
                    own(k_rope_ready)
                    for t in range(TT):
                        wait_done("uq", t, 0)
                        wait_done("uq", t, 1)
                        q3 = qtok[:, t * 768:(t + 1) * 768].rearrange("p (h d) -> p h d", h=8)
                        ct = cosv[:, t, :].unsqueeze(1).to_broadcast([P, 8, 16])
                        st = sinv[:, t, :].unsqueeze(1).to_broadcast([P, 8, 16])
                        tm = [rope_tmp[i // 2][:, 128 * (i % 2):128 * (i % 2) + 128].rearrange("p (h d) -> p h d", h=8)
                              for i in range(4)]
                        last = rope(q3[:, :, 64:80], q3[:, :, 80:96], q3[:, :, 64:80], q3[:, :, 80:96], ct, st, *tm)
                        if t == 0:
                            link(last)
                    last.then_inc(q_rope_ready, 1)
                    own(q_rope_ready)
                    b = wait_full("krt")
                    done(V.tensor_copy(kT_a[64:96, :].rearrange("p (h n) -> p h n", h=8),
                                       b[64:96, 0:T].unsqueeze(1).to_broadcast([32, 8, T])), "krt")
                    us = units(8)
                    n = len(us)
                    for i in range(n + 2):
                        if i < n:
                            t = us[i][2]
                            K = (t + 1) * P
                            b = wait_full("sb", "L", i)
                            L = unit_logits[i % 3][:, 0:2 * K].rearrange("p (h k) -> p h k", h=2)
                            done(V.tensor_tensor(L, b[:, 0:2 * K].rearrange("p (h k) -> p h k", h=2),
                                                 bias_of("strict", t).unsqueeze(1).to_broadcast([P, 2, K]), ALU.add),
                                 "sb", "L", i)
                        if 0 <= i - 1 < n:
                            K = (us[i - 1][2] + 1) * P
                            dve.wait_ge(softplus_done, i)
                            e = sb_e[(i - 1) % 2][:, 0:2 * K]
                            L = unit_logits[(i - 1) % 3][:, 0:2 * K]
                            suf = sb_suffix[:, 0:2 * K]
                            link(V.scalar_tensor_tensor(out=e, in0=L, scalar=0.0, in1=e, op0=ALU.max, op1=ALU.add))
                            m0 = 128 if K == 128 else 0
                            link(V.tensor_tensor_scan(suf[:, ::-1], suffix_mask[:, m0:m0 + 2 * K][:, ::-1], e[:, ::-1],
                                                      0.0, ALU.mult, ALU.add))
                            V.tensor_tensor(L, L, suf, ALU.subtract).then_inc(stick_arg_ready, 1)
                            own(stick_arg_ready)
                        if 0 <= i - 2 < n:
                            unit_output("sb", us, i - 2, 4)
                    softmax("mla", 8, 12, lambda t: bias_of("chunk", t), 96 ** -0.5, 0)
                else:
                    V.memset(dT, 0.0)
                    b = wait_full("ff")
                    done(V.tensor_scalar(f_y[0:16, :], b[0:16, 0:T], col("b_f")[0:16, :], None, ALU.add), "ff")
                    wait_done("ff")
                    dve.wait_ge(forget_ln_done, 1)
                    link(V.scalar_tensor_tensor(out=f_y[0:16, :], in0=f_y[0:16, :], scalar=0.0, in1=f_l[0:16, :],
                                                op0=ALU.min, op1=ALU.subtract))
                    V.tensor_tensor_scan(dT[0:16, :], ones[0:16, :], f_y[0:16, :], 0.0, ALU.mult, ALU.add)\
                        .then_inc(dcum_ready, 1)
                    own(dcum_ready)
                    b = wait_full("fd")
                    done(V.tensor_copy(dtok.rearrange("p (t h) -> p t h", t=2),
                                       b[:, 0:T].rearrange("p (t n) -> p t n", t=2)[:, :, 0:16]), "fd")
                    wait_done("fd")
                    softmax("fox", 16, 20, lambda t: bias_of("causal", t), 1.0, 0)
                layer_norm([((f"o{layer}_{n}", t), t, n) for n in range(2) for t in range(TT)], 0, 1,
                           f"ln1_{layer}", layer)
                for i in range(11):
                    b0 = wait_full(f"f13_{layer}_{i}", 0)
                    dve.wait_ge(silu_sig_done, 11 * layer + i + 1)
                    s = f_sig[i % 2]
                    done(V.tensor_tensor(s, b0[:, :], s, ALU.mult), f"f13_{layer}_{i}", 0)
                    wait_done(f"f13_{layer}_{i}", 0)
                    b1 = wait_full(f"f13_{layer}_{i}", 1)
                    done(V.tensor_tensor(hid[:, 2 * i * T:(2 * i + 2) * T], b1[:, :], s, ALU.mult),
                         f"f13_{layer}_{i}", 1)
                layer_norm([(("f2", layer, t, n), t, n) for t in range(TT) for n in range(2)], 2, 3,
                           f"ln2_{layer}", layer)
                order = [(n, t) for n in range(2) for t in range(TT)]
                for n, t in order:
                    b = wait_full(f"pg{layer}_{n}", t)
                    z = xn[:, n, t * 512:(t + 1) * 512]
                    done(V.tensor_tensor(z, b[:, :], lay_row(4)[:, n * 512:(n + 1) * 512], ALU.add), f"pg{layer}_{n}", t)
                for i, (n, t) in enumerate(order):
                    dve.wait_ge(ple_sig_done, 4 * layer + i + 1)
                    b = wait_full("pp", layer, n, t)
                    z = xn[:, n, t * 512:(t + 1) * 512]
                    done(V.tensor_tensor(z, b[:, :], z, ALU.mult), "pp", layer, n, t)
                    wait_done("pp", layer, n, t)
                    xs = x[:, t, n * 512:(n + 1) * 512]
                    last = V.tensor_tensor(xs, xs, z, ALU.add)
                if layer == 0:
                    last.then_inc(xn_ready, 1)
                    own(xn_ready)
                    evacuate("ple", None, None)
                else:
                    last.then_inc(x_done, 1)
                    own(x_done)


def _kn(w):
    k, n = w.shape
    return w.reshape(k // P, P, n).transpose(1, 0, 2).reshape(P, -1)


def _stream(i):
    import numpy as np
    parts = {}
    for j in range(12):
        parts[f"ada{j}"] = _kn(i["ada_w"][0][:, j * 512:(j + 1) * 512])
    w = i["w_in"][0]
    for name, a in [("hq", 0), ("hf", 512), ("hi", 1024), ("hg", 1536), ("sqk", 2048), ("sviq", 2560), ("cu", 3112)]:
        parts[name] = _kn(w[:, a:a + 512])
    for j in range(2):
        parts[f"wo{j}"] = _kn(i["w_out"][0][:, j * 512:(j + 1) * 512])
        parts[f"o0_{j}"] = _kn(i["a_w_out_2"][0][:, j * 512:(j + 1) * 512])
        parts[f"o1_{j}"] = _kn(i["c_w_out_2"][0][:, j * 512:(j + 1) * 512])
    for j in range(8):
        parts[f"m1_{j}"] = _kn(i["mlp_w1"][0][:, j * 512:(j + 1) * 512])
        parts[f"m2_{j}"] = _kn(i["mlp_w2"][0][j * 512:(j + 1) * 512, :])
    a = i["a_w_in_2"][0]
    parts["cqkv"] = _kn(a[:, 0:512])
    parts["sbq"], parts["sbk"], parts["sbv"] = (_kn(a[:, 544 + j * 512:544 + (j + 1) * 512]) for j in range(3))
    parts["lora"] = np.concatenate([_kn(i["a_w_uq_2"][0]), _kn(i["a_w_ukv_2"][0])], 1)
    c = i["c_w_in_2"][0]
    for j in range(2):
        parts[f"fq{j}"] = _kn(c[:, j * 512:(j + 1) * 512])
        parts[f"fk{j}"] = _kn(c[:, 1024 + j * 512:1024 + (j + 1) * 512])
        parts[f"fv{j}"] = _kn(c[:, 2048 + j * 512:2048 + (j + 1) * 512])
    for l in range(2):
        w1, w3, w2 = i["ffn_w1_2"][l], i["ffn_w3_2"][l], i["ffn_w2_2"][l]
        for j in range(11):
            s = slice(j * 256, (j + 1) * 256)
            parts[f"f13_{l}_{j}"] = np.concatenate([_kn(w1[:, s]), _kn(w3[:, s])], 1)
        at = 0
        for j, m in enumerate(FF2_TILES):
            parts[f"f2_{l}_{j}"] = _kn(w2[at * P:(at + m) * P, :])
            at += m
        for j in range(2):
            parts[f"pg{l}_{j}"] = _kn(i["ple_w_gate_2"][l][:, j * 512:(j + 1) * 512])
        parts[f"pp{l}"] = _kn(i["ple_w_proj_2"][l])
    out = np.zeros((len(STREAM), P, TILE), np.float32)
    for n, name in enumerate(STREAM):
        t = parts[name]
        out[n, :, 0:t.shape[1]] = t
    return out


def _constant_array():
    import numpy as np
    c = np.zeros((P, N_CONST), np.float32)
    q, s = np.arange(P)[:, None], np.arange(P)[None, :]

    def put(name, a, at=0):
        c[:, CONST[name] + at:CONST[name] + at + a.shape[1]] = a

    put("ident", (q == s).astype(np.float32))
    put("causal", np.where(s <= q, 0.0, NEG), P)
    put("strict", np.where(s < q, 0.0, NEG), P)
    put("chunk", np.where(s // 64 <= q // 64, 0.0, NEG), P)
    for l, b in enumerate(LEVELS):
        m = (q // (2 * b) == s // (2 * b)) & (q // b % 2 == 0) & (s // b % 2 == 1)
        put("levels", m.astype(np.float32), l * P)
    inv = (1.0 / (np.float32(10000.0) ** (np.arange(0, 32, 2, dtype=np.float32) / np.float32(32)))).astype(np.float32)
    ang = np.arange(T, dtype=np.float32)[:, None] * inv[None, :]
    put("cos", np.cos(ang).reshape(2, P, 16).transpose(1, 0, 2).reshape(P, 32))
    put("sin", np.sin(ang).reshape(2, P, 16).transpose(1, 0, 2).reshape(P, 32))
    put("negsel", -(q == s)[:, 0:16].astype(np.float32))
    return c


def kernel(**inputs):
    import numpy as np
    import concourse.bacc as bacc
    from concourse.bass_utils import run_bass_kernel_spmd

    i = {k: np.asarray(v) for k, v in inputs.items()}
    pcol = np.zeros((P, N_PCOL), np.float32)

    def put(name, v):
        v = np.asarray(v)
        pcol[:, PCOL[name]:PCOL[name] + v.size // P] = v.reshape(-1, P).T

    put("c", i["c"][0])
    put("ada_b", i["ada_b"][0])
    put("mix_w", i["norm_mix_w"][0])
    put("mlp_w", i["norm_mlp_w"][0])
    put("lb", i["hg_lb_logits"][0])
    put("onorm", i["hg_onorm_w"][0])
    put("cv_b", i["cv_b"][0])
    put("cv_ln_w", i["cv_ln_w"][0])
    put("cv_ln_b", i["cv_ln_b"][0])
    put("cv_w", i["cv_w"][0])
    put("fin_w", i["final_norm_w"])
    put("q_norm", i["a_q_norm_2"][0])
    put("kv_norm", i["a_kv_norm_2"][0])
    for l in range(2):
        for n in ("ln1_g", "ln1_b", "ln2_g", "ln2_b"):
            put(f"{n}{l}", i[f"{n}_2"][l])
    pcol[0:16, PCOL["b_f"]] = i["c_b_f_2"][0]
    prow = np.stack([i[f"{n}_2"][l] for l in range(2) for n in ("ln1_g", "ln1_b", "ln2_g", "ln2_b", "ple_b_gate")]
                    + [i["final_norm_w"]])
    w = i["w_in"][0]
    ik, iw = w[:, 3072:3104], w[:, 3104:3112]
    small = np.concatenate([_kn(np.concatenate([ik, ik, ik, ik, iw], 1)), _kn(i["c_w_in_2"][0][:, 3072:3088]),
                            _kn(i["a_w_in_2"][0][:, 512:544])], 1)
    pT = np.concatenate([_kn(np.ascontiguousarray(i["p_2"][l, 0].T)) for l in range(2)], 1)
    arrays = {
        "x": i["x"], "wstream": _stream(i), "wsmall": np.ascontiguousarray(small), "pcol": pcol,
        "prow": np.ascontiguousarray(prow), "const": _constant_array(), "p": np.ascontiguousarray(pT),
    }
    nc = bacc.Bacc("TRN2", target_bir_lowering=False, num_devices=1)
    args = [nc.dram_tensor(n, a.shape, F32, kind="ExternalInput").ap() for n, a in arrays.items()]
    out = nc.dram_tensor("out", (1, T, D), F32, kind="ExternalOutput").ap()
    build(nc, *args, out)
    r = run_bass_kernel_spmd(nc, [arrays], core_ids=[0])
    return r.results[0]["out"]
```

```python
import concourse.bass as bass
from concourse import mybir
from contextlib import ExitStack

F32 = mybir.dt.float32
ALU = mybir.AluOpType
ACT = mybir.ActivationFunctionType
AX = mybir.AxisListType

P = 128
T = 256
TT = T // P
D = 1024
DC = D // P
TILE = 2048
RAW, HI, LO = 3, 3, 2
F32R = mybir.dt.float32r
BANKS = 8
D_FF = 4096
D_FF_2 = 2816
ALPHA = 4.0 ** 0.25
EPS = 1e-6
EPS_LN = 1e-5
NEG = -1e30
TINY = 1e-30
TOPK = 64
LEVELS = [1, 2, 4, 8, 16, 32, 64]
LN_SPLIT = 2.0 ** 64

N_ADA = 24


def stream_names():
    def halves(*names):
        return [f"{n}.{j}" for n in names for j in range(2)]

    names = [f"ada{i}" for i in range(8)]
    names += halves("hf", "hq", "cu") + ["sv", "iq", "idx"] + halves("sqk", "hg", "hi")
    names += [f"ada{i}" for i in range(8, N_ADA)]
    names += halves("wo0", "wo1", *[f"m1_{i}" for i in range(8)]) + [f"m2_{i}" for i in range(16)]
    for layer in range(2):
        if layer == 0:
            names += halves("cqkv") + ["kr"] + halves("sbq", "sbk", "sbv") + ["uq", "ukv"]
        else:
            names += ["ff"] + halves("fq0", "fq1", "fk0", "fk1", "fv0", "fv1")
        names += halves(f"o{layer}_0", f"o{layer}_1")
        names += halves(*[f"f13_{layer}_{i}" for i in range(11)])
        names += [f"f2_{layer}_{i}" for i in range(11)]
        names += [f"pp{layer}"] + halves(f"pg{layer}_0", f"pg{layer}_1")
    return names


STREAM = stream_names()
SPLIT = [n for n in STREAM if not n.startswith("ada")]
SPLIT_NO = {n: i for i, n in enumerate(SPLIT)}
WIDTH = {"idx": DC * 136, "kr": DC * 32, "ff": DC * 16, "uq": 2 * 768}


def width(name):
    return WIDTH.get(name, TILE)


TILE_NO = {n: i for i, n in enumerate(STREAM)}

PCOL = {}


def _columns():
    at = 0
    for name, n in [("c", 8), ("ada_b", 48), ("mix_w", 8), ("mlp_w", 8), ("lb", 4), ("onorm", 4),
                    ("cv_b", 2), ("cv_ln_w", 2), ("cv_ln_b", 2), ("cv_w", 62), ("fin_w", 8),
                    ("q_norm", 2), ("kv_norm", 2), ("ln1_g0", 8), ("ln1_b0", 8), ("ln2_g0", 8),
                    ("ln2_b0", 8), ("ln1_g1", 8), ("ln1_b1", 8), ("ln2_g1", 8), ("ln2_b1", 8),
                    ("b_f", 1)]:
        PCOL[name] = at
        at += n
    return at


N_PCOL = _columns()

CONST = {}


def _constants():
    at = 0
    for name, n in [("ident", 128), ("causal", 256), ("strict", 256), ("chunk", 256),
                    ("levels", 128 * len(LEVELS)), ("cos", 32), ("sin", 32), ("negsel", 16)]:
        CONST[name] = at
        at += n
    return at


N_CONST = _constants()


def units(heads):
    return [(g, par, t) for g in range(heads // 4) for t in range(TT) for par in range(2)]


def unit_order(name, n):
    order = []
    for i in range(n + 3):
        if i < n:
            order.append((name, "L", i))
        if 0 <= i - 2 < n:
            order.append((name, "T", i - 2))
        if 0 <= i - 3 < n:
            order.append((name, "O", i - 3))
    return order


def psum_plan():
    plan = [("mod", u) for u in range(4)]

    def transposes(stage):
        plan.extend([("tr", stage, j) for j in range(4)])

    def gemm(name):
        plan.extend([(name, 0), (name, 1)])

    def level(lv):
        plan.extend([("lev", lv, 0), ("lev", lv, 1)])

    transposes("mix")
    gemm("hf")
    gemm("hq")
    gemm("cu")
    plan.append(("sv",))
    plan.append(("iq",))
    plan.extend([("ik",), ("iw",)])
    level(0)
    level(1)
    gemm("sqk")
    level(2)
    level(3)
    gemm("hg")
    level(4)
    level(5)
    gemm("hi")
    level(6)
    level(7)
    plan.append(("lev", 8, 0))
    plan.extend([("sc", t, j) for t in range(TT) for j in range(4)])
    plan.extend([("mod", u) for u in range(4, N_ADA // 2)])
    plan.extend([("hgo", 0), ("hgo", 1)])
    plan.append(("cmean",))
    plan.append(("cvar",))
    plan.extend([("hgt", 0), ("hgt", 1)])
    plan.extend(unit_order("dsa", 4))
    gemm("wo0")
    gemm("wo1")
    transposes("mlp")
    for i in range(8):
        gemm(f"m1_{i}")
    plan.extend([("m2", t, n) for t in range(TT) for n in range(2)])
    transposes("fin")
    for layer in range(2):
        if layer == 0:
            gemm("cqkv")
            plan.append(("kr",))
            gemm("sbq")
            gemm("sbk")
            gemm("sbv")
            plan.extend([("ct", 0), ("ct", 1)])
            plan.extend([("uq", t, n) for t in range(TT) for n in range(2)])
            plan.extend([("uk", j) for j in range(4)])
            plan.extend([("uv", n) for n in range(2)])
            plan.append(("krt",))
            plan.extend(unit_order("sb", 8))
            plan.extend([("qt", j) for j in range(4)])
            plan.extend(unit_order("mla", 8))
        else:
            plan.append(("ff",))
            for n in ["fq0", "fq1", "fk0", "fk1", "fv0", "fv1"]:
                gemm(n)
            plan.append(("fd",))
            plan.extend(unit_order("fox", 16))
        gemm(f"o{layer}_0")
        gemm(f"o{layer}_1")
        transposes(f"ln1_{layer}")
        for i in range(11):
            gemm(f"f13_{layer}_{i}")
        plan.extend([("f2", layer, t, n) for t in range(TT) for n in range(2)])
        transposes(f"ln2_{layer}")
        plan.extend([("pp", layer, n) for n in range(4)])
        gemm(f"pg{layer}_0")
        gemm(f"pg{layer}_1")
        if layer == 0:
            transposes("ple")
    return plan


PLAN = psum_plan()
USE = {key: i for i, key in enumerate(PLAN)}
assert len(USE) == len(PLAN)


def full(*key):
    return USE[key] + 1


def bank(*key):
    return USE[key] % BANKS


def read(*key):
    return USE[key] // BANKS + 1


def build(nc, x_in, wstream, pcol_in, prow_in, const_in, p_in, out):
    ctx = ExitStack()
    with ctx:
        def sb(name, shape):
            return ctx.enter_context(nc.sbuf_tensor(name, shape, F32))

        def sem(name):
            return ctx.enter_context(nc.semaphore(name))

        arena_at = (nc.sbuf_base + 31) // 32 * 32
        ARENA = 20672
        arena = sb("arena", [P, ARENA])

        def rounded(name, n, offset=None):
            if offset is None:
                return ctx.enter_context(nc.sbuf_tensor(name, [P, n], F32R))
            return nc.alloc_sbuf_tensor_at(name, [P, n], F32R, offset=arena_at + 4 * offset)

        raw = sb("raw", [P, RAW, TILE])
        w_hi = [rounded(f"w_hi{i}", TILE) for i in range(HI)]
        w_lo = [rounded(f"w_lo{i}", TILE) for i in range(LO)]
        x = sb("x_res", [P, TT, D])
        xn = sb("xn", [P, TT, D])
        hT_hi, hT_lo = rounded("hT_hi", DC * T), rounded("hT_lo", DC * T)
        mixT = sb("mixT", [P, DC, T])
        rows = sb("rows", [P, 2, D])
        pcol = sb("pcol_sb", [P, N_PCOL])
        const = sb("const_sb", [P, N_CONST])
        pT = sb("pT", [P, 2, 2, T])
        ones = sb("ones", [P, T])
        avg = sb("avg", [P, P])
        tiny = sb("tiny", [P, 256])

        top = [0]

        def cut(n):
            a = arena[:, top[0]:top[0] + n]
            top[0] += n
            assert top[0] <= ARENA, top[0]
            return a

        psum = [ctx.enter_context(nc.psum_tensor(f"bank{i}", [P, 512], F32)) for i in range(BANKS)]

        def ps(*key):
            return psum[bank(*key)]

        def col(name, i=0, n=1):
            return pcol[:, PCOL[name] + i:PCOL[name] + i + n]

        ident = const[:, CONST["ident"]:CONST["ident"] + P]

        def bias_of(kind, t):
            at = CONST[kind]
            return const[:, at + P:at + 2 * P] if t == 0 else const[:, at:at + 2 * P]

        unit_logits = [cut(512) for _ in range(4)]
        unit_probsT = [cut(512) for _ in range(2)]
        fresh = arena[:, 0:2048]
        unit_base = top[0]
        q_hg, k_hg, G_hg = cut(1024), cut(1024), cut(1024)
        QK = [cut(1024), cut(1024)]
        E_hg = [xn[:, 0, :], xn[:, 1, :]]
        sg_hg, A_hg, A1_hg, v_hg = cut(1024), cut(1024), cut(512), cut(1024)
        lev_tmp = [cut(512), cut(512)]
        sqT, skT, iqT, sv = cut(512), cut(512), cut(512), cut(512)
        ikT = cut(256)
        iw = cut(16)
        relu = [cut(512), cut(512)]
        score = [cut(256), cut(256)]
        score_left = cut(256)
        sel_bias = [cut(256), cut(256)]
        picks = cut(256)
        m8 = cut(8)
        hpad = cut(2 * 286)
        conv = cut(512)
        conv_d = cut(512)
        gate_tmp = lev_tmp
        hid_hi, hid_lo = rounded("hid_hi", 32 * T, unit_base), rounded("hid_lo", 32 * T, unit_base + 32 * T)
        hid2_hi, hid2_lo = rounded("hid2_hi", 22 * T, unit_base), rounded("hid2_lo", 22 * T, unit_base + 22 * T)
        g2_at = max(unit_base + 64 * T, top[0])
        g2_row = arena[:, g2_at:g2_at + D]
        assert g2_at + D <= ARENA
        act_out, product = unit_logits[0:2], unit_logits[2:4]
        res_tmp = unit_probsT
        top[0] = unit_base
        qtok = cut(TT * 768)
        rope_tmp = [cut(256), cut(256)]
        krtok = cut(TT * 96)
        qT_a, kT_a, v_a = cut(2048), cut(2048), cut(1024)
        qT_b, kT_b, v_b = cut(1024), cut(1024), cut(1024)
        sb_e = [cut(512), cut(512)]
        sb_suffix = cut(512)
        suffix_mask = cut(512)
        assert top[0] >= unit_base + 44 * T
        lay = cut(5 * D)
        top[0] = unit_base
        qT_c, kT_c, v_c = cut(2048), cut(2048), cut(2048)
        dT, dtok = cut(256), cut(32)
        f_y, f_l = cut(256), cut(256)

        csil = tiny[:, 0:8]
        mod = tiny[:, 8:56]
        norm_a = tiny[:, 56:64]
        lb = tiny[:, 64:68]
        one_lb = tiny[:, 68:72]
        ssum = tiny[:, 72:80]
        stat = tiny[:, 80:96]
        root = tiny[:, 96:104]
        negmax = tiny[:, 104:112]
        rowsum = tiny[:, 112:120]
        rinv = tiny[:, 120:128]
        need = tiny[:, 128:130]
        count = tiny[:, 130:132]
        lbw = tiny[:, 132:140]
        bn = tiny[:, 140:164]
        mv = tiny[:, 164:172]
        zero8 = tiny[:, 172:180]

        h4 = lambda a: a.rearrange("p (h n) -> p h n", h=4)

        def lay_row(i):
            return lay[:, i * D:(i + 1) * D]

        weights_loaded = [sem(f"weights_loaded{i}") for i in range(RAW)]
        weights_rounded = sem("weights_rounded")
        weights_split = sem("weights_split")
        weights_started = sem("weights_started")
        ada_used = sem("ada_used")
        p_split = sem("p_split")
        input_split = sem("input_split")
        hid_split = sem("hid_split")
        psum_full = sem("psum_full")
        bank_read = [sem(f"bank_read{i}") for i in range(BANKS)]
        x_loaded, pcol_loaded, const_loaded = sem("x_loaded"), sem("pcol_loaded"), sem("const_loaded")
        p_loaded, rows_loaded = sem("p_loaded"), sem("rows_loaded")
        lay_loaded = sem("lay_loaded")
        dve_step, act_step, pool_step = sem("dve_step"), sem("act_step"), sem("pool_step")
        lb_diff_ready, lb_exp_done = sem("lb_diff_ready"), sem("lb_exp_done")
        x_res_ready = sem("x_res_ready")
        c_sig_done, c_ready = sem("c_sig_done"), sem("c_ready")
        squares_summed, root_ready, var_ready = sem("squares_summed"), sem("root_ready"), sem("var_ready")
        xn_ready = sem("xn_ready")
        norm_coef_ready = sem("norm_coef_ready")
        hf_sig_done, f_clipped, logs_done = sem("hf_sig_done"), sem("f_clipped"), sem("logs_done")
        hq_sig_done, hg_sig_done = sem("hq_sig_done"), sem("hg_sig_done")
        conv_done = sem("conv_done")
        conv_sq_ready = sem("conv_sq_ready")
        conv_scaled, conv_sig_done, conv_out_ready = sem("conv_scaled"), sem("conv_sig_done"), sem("conv_out_ready")
        decay_arg_ready, decay_exp_done, qk_ready = sem("decay_arg_ready"), sem("decay_exp_done"), sem("qk_ready")
        levels_summed, o_normed = sem("levels_summed"), sem("o_normed")
        gate_bias_loaded = sem("gate_bias_loaded")
        relu_used = sem("relu_used")
        logits_ready, exp_done, probs_ready = sem("logits_ready"), sem("exp_done"), sem("probs_ready")
        softplus_done, stick_arg_ready = sem("softplus_done"), sem("stick_arg_ready")
        stick_probs_ready = sem("stick_probs_ready")
        silu_sig_done = sem("silu_sig_done")
        q_rope_ready, k_rope_ready = sem("q_rope_ready"), sem("k_rope_ready")
        c_normed = sem("c_normed")
        ple_sig_done = sem("ple_sig_done")
        forget_ln_done, dcum_ready = sem("forget_ln_done"), sem("dcum_ready")
        x_done, out_stored = sem("x_done"), sem("out_stored")

        block = ctx.enter_context(nc.Block())

        @block.sync
        def _(sp):
            for i, name in enumerate(STREAM):
                if i >= RAW:
                    before = STREAM[i - RAW]
                    if before in SPLIT_NO:
                        sp.wait_ge(weights_split, SPLIT_NO[before] + 1)
                    elif int(before[3:]) % 2 == 0:
                        sp.wait_ge(ada_used, int(before[3:]) // 2 + 1)
                    else:
                        sp.wait_ge(psum_full, full("mod", int(before[3:]) // 2))
                sp.dma_start(raw[:, i % RAW, 0:width(name)], wstream[i, :, 0:width(name)])\
                    .then_inc(weights_loaded[i % RAW], 16)
            sp.wait_ge(x_done, 1)
            sp.dma_start(out.rearrange("o (t p) d -> p (o t) d", p=P), x[:, :, :])\
                .then_inc(out_stored, 16)
            sp.wait_ge(out_stored, 16)

        @block.tensor
        def _(pe):
            mm = nc.tensor.matmul
            at = [0]

            def begin(*key):
                assert PLAN[at[0]] == key, (PLAN[at[0]], key)
                at[0] += 1
                u = USE[key]
                if u >= BANKS:
                    pe.wait_ge(bank_read[u % BANKS], u // BANKS)
                return psum[u % BANKS]

            def in_sbuf(*key):
                pe.wait_ge(bank_read[bank(*key)], read(*key))

            def tile(name):
                n = SPLIT_NO[name]
                pe.wait_ge(weights_split, n + 1)
                return w_hi[n % HI][:, 0:width(name)], w_lo[n % LO][:, 0:width(name)], [True]

            def product3(o, a, b, start, stop, first):
                ins = mm(o, a[0], b[0], start=start, stop=False)
                if first[0]:
                    ins.then_inc(weights_started, 1)
                    first[0] = False
                mm(o, a[0], b[1], start=False, stop=False)
                return mm(o, a[1], b[0], start=False, stop=stop)

            splits = [0]

            def chunks(n):
                splits[0] += n // 2

            def x_part(k, lo=0, hi=T):
                return hT_hi[:, k * T + lo:k * T + hi], hT_lo[:, k * T + lo:k * T + hi]

            def x_ready(k, n=DC):
                pe.wait_ge(input_split, splits[0] - n // 2 + k // 2 + 1)

            def feature_half(name, o_width=P, n_out=2, at_=0, key=None, kn=None):
                wh, wl, first = tile(name) if kn is None else kn
                vh, vl = (w.rearrange("p (k n) -> p k n", k=DC) for w in (wh, wl))
                b = begin(*key)
                for o in range(n_out):
                    for k in range(DC):
                        c = at_ + o * o_width
                        x_ready(k)
                        last = product3(b[0:o_width, o * T:(o + 1) * T],
                                        (vh[:, k, c:c + o_width], vl[:, k, c:c + o_width]), x_part(k),
                                        k == 0, k == DC - 1, first)
                last.then_inc(psum_full, 1)

            def token_half(name, n, at_=0, key=None, kn=None):
                wh, wl, first = tile(name) if kn is None else kn
                vh, vl = (w.rearrange("p (k n) -> p k n", k=DC) for w in (wh, wl))
                b = begin(*key)
                for t in range(TT):
                    for k in range(DC):
                        x_ready(k)
                        last = product3(b[:, t * n:(t + 1) * n], x_part(k, t * P, (t + 1) * P),
                                        (vh[:, k, at_:at_ + n], vl[:, k, at_:at_ + n]),
                                        k == 0, k == DC - 1, first)
                last.then_inc(psum_full, 1)

            def gemm_feature(name):
                for j in range(2):
                    feature_half(f"{name}.{j}", key=(name, j))

            def gemm_token(name):
                for j in range(2):
                    token_half(f"{name}.{j}", T, key=(name, j))

            def to_feature_form(stage, n):
                pe.wait_ge(xn_ready, n)
                for j in range(4):
                    b = begin("tr", stage, j)
                    for c in range(2):
                        for t in range(TT):
                            last = nc.tensor.transpose(
                                b[:, c * T + t * P:c * T + (t + 1) * P],
                                (x if stage == "ple" else xn)[:, t, (2 * j + c) * P:(2 * j + c + 1) * P], ident)
                    last.then_inc(psum_full, 1)
                chunks(DC)

            def modulation(u):
                b = begin("mod", u)
                for j in range(2):
                    slot = TILE_NO[f"ada{2 * u + j}"]
                    pe.wait_ge(weights_loaded[slot % RAW], 16 * (slot // RAW + 1))
                    w = raw[:, slot % RAW, :].rearrange("p (k n) -> p k n", k=DC)
                    for k in range(DC):
                        last = mm(b[:, j * T:(j + 1) * T], csil[:, k:k + 1].to_broadcast([P, P]), w[:, k, :],
                                  start=k == 0, stop=k == DC - 1)
                    last.then_inc(psum_full if j else ada_used, 1)

            def decay_level(lv):
                pe.wait_ge(qk_ready, lv + 1)
                for j in range(1 if lv == 8 else 2):
                    b = begin("lev", lv, j)
                    for i in range(4):
                        if lv == 8:
                            at_ = i * T
                            lhsT, rhs = QK[lv % 2][:, at_:at_ + P], QK[lv % 2][:, at_ + P:at_ + T]
                        else:
                            at_ = (4 * j + i) * P
                            lhsT = rhs = QK[lv % 2][:, at_:at_ + P]
                            if lv == 0:
                                lhsT, rhs = k_hg[:, at_:at_ + P], q_hg[:, at_:at_ + P]
                        last = mm(b[:, i * P:(i + 1) * P], lhsT, rhs, start=True, stop=True)
                    last.then_inc(psum_full, 1)

            def attention(name, heads, logits, values, probs, base):
                us = units(heads)
                for key in unit_order(name, len(us)):
                    _, what, i = key
                    g, par, t = us[i]
                    nb = t + 1
                    K = nb * P
                    b = begin(*key)
                    if what == "L":
                        for hh in range(2):
                            last = logits(b[:, hh * K:(hh + 1) * K], 4 * g + par + 2 * hh, t, K)
                    elif what == "T":
                        pe.wait_ge(probs, base + i + 1)
                        p_ = unit_logits[i % 4]
                        for m in range(2 * nb):
                            last = nc.tensor.transpose(b[:, m * P:(m + 1) * P],
                                                       p_[:, m * P:(m + 1) * P], ident)
                    else:
                        in_sbuf(name, "T", i)
                        pT_ = unit_probsT[i % 2]
                        for hh in range(2):
                            for m in range(nb):
                                last = mm(b[par * 64:par * 64 + 64, hh * P:(hh + 1) * P],
                                          values(4 * g + par + 2 * hh, m),
                                          pT_[:, (hh * nb + m) * P:(hh * nb + m + 1) * P],
                                          start=m == 0, stop=m == nb - 1)
                    last.then_inc(psum_full, 1)

            def two_in_rows(qT, kT):
                def logits(o, h, t, K):
                    r = (h % 2) * 64
                    c = (h // 2) * T
                    return mm(o, qT[r:r + 64, c + t * P:c + (t + 1) * P], kT[r:r + 64, c:c + K],
                              start=True, stop=True)
                return logits

            pe.wait_ge(c_ready, 1)
            for u in range(4):
                modulation(u)
            pe.wait_ge(const_loaded, 16)
            to_feature_form("mix", 1)
            gemm_feature("hf")
            gemm_feature("hq")
            gemm_feature("cu")
            token_half("sv", T, key=("sv",))
            feature_half("iq", key=("iq",))
            kn = tile("idx")
            feature_half("idx", n_out=1, key=("ik",), kn=kn)
            token_half("idx", 8, at_=P, key=("iw",), kn=kn)
            decay_level(0)
            decay_level(1)
            gemm_feature("sqk")
            decay_level(2)
            decay_level(3)
            gemm_feature("hg")
            decay_level(4)
            decay_level(5)
            gemm_token("hi")
            decay_level(6)
            decay_level(7)
            decay_level(8)
            in_sbuf("iq")
            in_sbuf("ik")
            for t in range(TT):
                K = (t + 1) * P
                for j in range(4):
                    b = begin("sc", t, j)
                    r = 32 * j
                    for hh in range(2):
                        last = mm(b[:, hh * K:(hh + 1) * K],
                                  iqT[r:r + 32, hh * T + t * P:hh * T + (t + 1) * P],
                                  ikT[r:r + 32, 0:K], start=True, stop=True)
                    last.then_inc(psum_full, 1)
            for u in range(4, N_ADA // 2):
                modulation(u)
            pe.wait_ge(levels_summed, 1)
            in_sbuf("hi", 0)
            in_sbuf("hi", 1)
            in_sbuf("lev", 8, 0)
            b = begin("hgo", 0)
            for h in range(4):
                last = mm(b[:, h * P:(h + 1) * P], A_hg[:, h * T:h * T + P], v_hg[:, h * P:(h + 1) * P],
                          start=True, stop=True)
            last.then_inc(psum_full, 1)
            b = begin("hgo", 1)
            for h in range(4):
                mm(b[:, h * P:(h + 1) * P], A1_hg[:, h * P:(h + 1) * P], v_hg[:, h * P:(h + 1) * P],
                   start=True, stop=False)
                last = mm(b[:, h * P:(h + 1) * P], A_hg[:, h * T + P:(h + 1) * T],
                          v_hg[:, 512 + h * P:512 + (h + 1) * P], start=False, stop=True)
            last.then_inc(psum_full, 1)
            pe.wait_ge(conv_done, 1)
            b = begin("cmean")
            for c in range(2):
                last = mm(b[:, 0:T], avg[:, :], conv[:, c * T:(c + 1) * T], start=c == 0, stop=c == 1)
            last.then_inc(psum_full, 1)
            pe.wait_ge(conv_sq_ready, 1)
            b = begin("cvar")
            for c in range(2):
                last = mm(b[:, 0:T], avg[:, :], conv[:, c * T:(c + 1) * T], start=c == 0, stop=c == 1)
            last.then_inc(psum_full, 1)
            for t in range(TT):
                pe.wait_ge(o_normed, t + 1)
                b = begin("hgt", t)
                for h in range(4):
                    last = nc.tensor.transpose(b[:, h * P:(h + 1) * P],
                                               q_hg[:, t * 512 + h * P:t * 512 + (h + 1) * P], ident)
                last.then_inc(psum_full, 1)
            in_sbuf("sqk", 0)
            in_sbuf("sqk", 1)
            in_sbuf("sv")
            attention("dsa", 4, two_in_rows(sqT, skT),
                      lambda h, m: sv[:, m * T + h * 64:m * T + (h + 1) * 64], probs_ready, 0)
            chunks(DC)
            gemm_token("wo0")
            gemm_token("wo1")
            to_feature_form("mlp", 2)
            for i in range(8):
                gemm_feature(f"m1_{i}")

            def down(key, names, hi_, lo_, base):
                banks = {(t, n): begin(*key, t, n) for t in range(TT) for n in range(2)}
                total = 2 * len(names)
                for q, name in enumerate(names):
                    wh, wl, first = tile(name)
                    pe.wait_ge(hid_split, base + q + 1)
                    for i in range(2):
                        c = 2 * q + i
                        for t in range(TT):
                            for n in range(2):
                                a = c * T + t * P
                                s = slice(i * D + n * 512, i * D + (n + 1) * 512)
                                last = product3(banks[t, n][:, :], (hi_[:, a:a + P], lo_[:, a:a + P]),
                                                (wh[:, s], wl[:, s]), c == 0, c == total - 1, first)
                                if c == total - 1:
                                    last.then_inc(psum_full, 1)

            down(("m2",), [f"m2_{i}" for i in range(16)], hid_hi, hid_lo, 0)
            to_feature_form("fin", 3)
            xn_count = 3
            for layer in range(2):
                if layer == 0:
                    gemm_token("cqkv")
                    token_half("kr", 32, key=("kr",))
                    gemm_feature("sbq")
                    gemm_feature("sbk")
                    gemm_token("sbv")
                    for j in range(2):
                        if j == 0:
                            pe.wait_ge(c_normed, 1)
                        b = begin("ct", j)
                        for c in range(2):
                            for t in range(TT):
                                last = nc.tensor.transpose(
                                    b[:, c * T + t * P:c * T + (t + 1) * P],
                                    xn[:, t, (2 * j + c) * P:(2 * j + c + 1) * P], ident)
                        last.then_inc(psum_full, 1)
                    chunks(4)
                    wh, wl, first = tile("uq")
                    vh, vl = (w.rearrange("p (k n) -> p k n", k=2) for w in (wh, wl))
                    for t in range(TT):
                        for n in range(2):
                            b = begin("uq", t, n)
                            m = 512 if n == 0 else 256
                            for k in range(2):
                                x_ready(k, 4)
                                last = product3(b[:, 0:m], x_part(k, t * P, (t + 1) * P),
                                                (vh[:, k, n * 512:n * 512 + m], vl[:, k, n * 512:n * 512 + m]),
                                                k == 0, k == 1, first)
                            last.then_inc(psum_full, 1)
                    wh, wl, first = tile("ukv")
                    vh, vl = (w.rearrange("p (k n) -> p k n", k=2) for w in (wh, wl))
                    for j in range(4):
                        b = begin("uk", j)
                        for o in range(2):
                            for k in range(2):
                                x_ready(2 + k, 4)
                                c = (2 * j + o) * 64
                                last = product3(b[0:64, o * T:(o + 1) * T], (vh[:, k, c:c + 64], vl[:, k, c:c + 64]),
                                                x_part(2 + k), k == 0, k == 1, first)
                        last.then_inc(psum_full, 1)
                    for n in range(2):
                        b = begin("uv", n)
                        for t in range(TT):
                            for k in range(2):
                                c = 512 + n * T
                                last = product3(b[:, t * T:(t + 1) * T], x_part(2 + k, t * P, (t + 1) * P),
                                                (vh[:, k, c:c + T], vl[:, k, c:c + T]), k == 0, k == 1, first)
                        last.then_inc(psum_full, 1)
                    pe.wait_ge(k_rope_ready, 1)
                    b = begin("krt")
                    for t in range(TT):
                        last = nc.tensor.transpose(b[0:96, t * P:(t + 1) * P], krtok[:, t * 96:(t + 1) * 96], ident)
                    last.then_inc(psum_full, 1)
                    for n_ in ("sbq", "sbk", "sbv"):
                        in_sbuf(n_, 0)
                        in_sbuf(n_, 1)
                    attention("sb", 8, two_in_rows(qT_b, kT_b),
                              lambda h, m: v_b[:, m * 512 + h * 64:m * 512 + (h + 1) * 64], stick_probs_ready, 0)
                    pe.wait_ge(q_rope_ready, 1)
                    for j in range(4):
                        b = begin("qt", j)
                        for o in range(2):
                            for t in range(TT):
                                h = 2 * j + o
                                last = nc.tensor.transpose(
                                    b[0:96, o * T + t * P:o * T + (t + 1) * P],
                                    qtok[:, t * 768 + h * 96:t * 768 + (h + 1) * 96], ident)
                        last.then_inc(psum_full, 1)
                    for j in range(4):
                        in_sbuf("qt", j)
                        in_sbuf("uk", j)
                    in_sbuf("krt")
                    in_sbuf("uv", 0)
                    in_sbuf("uv", 1)

                    def mla_logits(o, h, t, K):
                        return mm(o, qT_a[0:96, h * T + t * P:h * T + (t + 1) * P],
                                  kT_a[0:96, h * T:h * T + K], start=True, stop=True)
                    attention("mla", 8, mla_logits,
                              lambda h, m: v_a[:, m * 512 + h * 64:m * 512 + (h + 1) * 64], probs_ready, 4)
                else:
                    feature_half("ff", o_width=16, n_out=1, key=("ff",))
                    for n_ in ["fq0", "fq1", "fk0", "fk1"]:
                        gemm_feature(n_)
                    gemm_token("fv0")
                    gemm_token("fv1")
                    pe.wait_ge(dcum_ready, 1)
                    b = begin("fd")
                    for t in range(TT):
                        last = nc.tensor.transpose(b[:, t * P:(t + 1) * P], dT[:, t * P:(t + 1) * P], ident)
                    last.then_inc(psum_full, 1)
                    for n_ in ["fq0", "fq1", "fk0", "fk1", "fv0", "fv1"]:
                        in_sbuf(n_, 0)
                        in_sbuf(n_, 1)
                    plain = two_in_rows(qT_c, kT_c)
                    negsel = const[:, CONST["negsel"]:CONST["negsel"] + 16]

                    def fox_logits(o, h, t, K):
                        r = (h % 2) * 64
                        c = (h // 2) * T
                        mm(o, negsel[:, h:h + 1].to_broadcast([P, P]), dT[:, 0:K], start=True, stop=False)
                        return mm(o, qT_c[r:r + 64, c + t * P:c + (t + 1) * P], kT_c[r:r + 64, c:c + K],
                                  start=False, stop=True)
                    attention("fox", 16, fox_logits,
                              lambda h, m: v_c[:, m * D + h * 64:m * D + (h + 1) * 64], probs_ready, 12)
                chunks(DC)
                gemm_token(f"o{layer}_0")
                gemm_token(f"o{layer}_1")
                xn_count += 1
                to_feature_form(f"ln1_{layer}", xn_count)
                for i in range(11):
                    gemm_feature(f"f13_{layer}_{i}")
                down(("f2", layer), [f"f2_{layer}_{i}" for i in range(11)], hid2_hi, hid2_lo, 16 + 11 * layer)
                xn_count += 1
                to_feature_form(f"ln2_{layer}", xn_count)
                wh, wl, first = tile(f"pp{layer}")
                vh, vl = (w.rearrange("p (k n) -> p k n", k=2) for w in (wh, wl))
                pe.wait_ge(p_split, layer + 1)
                for n_ in range(4):
                    b = begin("pp", layer, n_)
                    for t in range(TT):
                        for k in range(2):
                            a = k * T + t * P
                            last = product3(b[:, t * T:(t + 1) * T], (hid2_hi[:, a:a + P], hid2_lo[:, a:a + P]),
                                            (vh[:, k, n_ * T:(n_ + 1) * T], vl[:, k, n_ * T:(n_ + 1) * T]),
                                            k == 0, k == 1, first)
                    last.then_inc(psum_full, 1)
                for i in range(2):
                    gemm_token(f"pg{layer}_{i}")
                if layer == 0:
                    xn_count += 1
                    to_feature_form("ple", xn_count)

        @block.scalar
        def _(act):
            step = [0]
            A = nc.scalar.activation

            def link(ins):
                step[0] += 1
                ins.then_inc(act_step, 1)
                act.wait_ge(act_step, step[0])

            def wait_full(*key):
                act.wait_ge(psum_full, full(*key))
                return ps(*key)

            def done(ins, *key):
                ins.then_inc(bank_read[bank(*key)], 1)

            def rms_squares(n):
                for t in range(TT):
                    last = A(xn[:, t, :], x[:, t, :], ACT.Square, accum_out=ssum[:, t:t + 1])
                last.then_inc(squares_summed, 1)

            def square_root(width, n):
                act.wait_ge(var_ready, n)
                A(root[:, 0:width], stat[:, 0:width], ACT.Sqrt).then_inc(root_ready, 1)

            def evacuate(stage, scale, shift):
                for j in range(4):
                    b = wait_full("tr", stage, j)
                    for c in range(2):
                        f = 2 * j + c
                        dst = fresh[:, f * T:(f + 1) * T]
                        if scale is None:
                            last = A(dst, b[:, c * T:(c + 1) * T], ACT.Copy)
                        else:
                            last = A(dst, b[:, c * T:(c + 1) * T], ACT.Identity,
                                     scale=scale[:, f:f + 1], bias=shift[:, f:f + 1])
                    done(last, "tr", stage, j)

            next_hi = [0]

            def ahead(name, by=2, last=len(SPLIT) - 1):
                while next_hi[0] <= min(SPLIT_NO[name] + by, last):
                    n = next_hi[0]
                    slot = TILE_NO[SPLIT[n]]
                    act.wait_ge(weights_loaded[slot % RAW], 16 * (slot // RAW + 1))
                    if n >= HI:
                        act.wait_ge(weights_started, n - HI + 2)
                    m = width(SPLIT[n])
                    A(w_hi[n % HI][:, 0:m], raw[:, slot % RAW, 0:m], ACT.Copy).then_inc(weights_rounded, 1)
                    next_hi[0] += 1

            def bank_of(name, *key):
                w_in_end = SPLIT_NO["hi.1"]
                ahead(name, last=w_in_end if SPLIT_NO[name] <= w_in_end else len(SPLIT) - 1)
                return wait_full(*key)

            def softmax(name, heads, base):
                us = units(heads)
                for i in range(len(us) + 2):
                    if i < len(us):
                        K = (us[i][2] + 1) * P
                        act.wait_ge(logits_ready, base + i + 1)
                        m = 2 * (i % 4)
                        for hh in range(2):
                            L = unit_logits[i % 4][:, hh * K:(hh + 1) * K]
                            last = A(L, L, ACT.Exp, bias=negmax[:, m + hh:m + hh + 1],
                                     accum_out=rowsum[:, m + hh:m + hh + 1])
                        last.then_inc(exp_done, 1)
                    if i >= 2:
                        transposed(name, us, i - 2)

            def transposed(name, us, i):
                K = (us[i][2] + 1) * P
                b = wait_full(name, "T", i)
                if i >= 2:
                    act.wait_ge(psum_full, full(name, "O", i - 2))
                done(A(unit_probsT[i % 2][:, 0:2 * K], b[:, 0:2 * K], ACT.Copy), name, "T", i)

            act.dma_start(pcol[:, :], pcol_in).then_inc(pcol_loaded, 16)
            act.dma_start(x[:, :, :], x_in.rearrange("o (t p) d -> p (o t) d", p=P)).then_inc(x_loaded, 16)
            act.dma_start(const[:, :], const_in).then_inc(const_loaded, 16)
            act.dma_start(rows[:, 0, :], prow_in[10, :].partition_broadcast(P)).then_inc(rows_loaded, 16)
            for i, row in enumerate((rows[:, 1, :], g2_row)):
                act.dma_start(row, prow_in[11 + i, :].partition_broadcast(P)).then_inc(gate_bias_loaded, 16)
            act.dma_start(pT[:, :, :, :], p_in.rearrange("p (l k n) -> p l k n", l=2, k=2)).then_inc(p_loaded, 16)
            act.wait_ge(pcol_loaded, 16)
            A(csil, col("c", 0, 8), ACT.Sigmoid).then_inc(c_sig_done, 1)
            act.wait_ge(lb_diff_ready, 1)
            A(lbw[:, 0:4], lbw[:, 0:4], ACT.Exp).then_inc(lb_exp_done, 1)
            act.wait_ge(x_loaded, 16)
            rms_squares(1)
            square_root(TT, 1)
            act.wait_ge(norm_coef_ready, 1)
            ahead("hf.0", 1)
            evacuate("mix", norm_a, mod[:, 0:8])
            for j in range(2):
                b = bank_of(f"hf.{j}", "hf", j)
                A(G_hg[:, j * 512:(j + 1) * 512], b[:, :], ACT.Sigmoid)
                last = A(k_hg[:, j * 512:(j + 1) * 512], b[:, :], ACT.Sigmoid, scale=-1.0)
                done(last, "hf", j)
            for j in range(2):
                b = bank_of(f"hq.{j}", "hq", j)
                A(q_hg[:, j * 512:(j + 1) * 512], b[:, :], ACT.Sigmoid).then_inc(hq_sig_done, 1)
            ahead("cu.0")
            act.wait_ge(f_clipped, 1)
            A(G_hg, G_hg, ACT.Ln)
            A(QK[0], QK[0], ACT.Ln).then_inc(logs_done, 1)
            b = bank_of("cu.1", "cu", 1)
            done(A(conv_d, b[:, :], ACT.Sigmoid), "cu", 1)
            b = bank_of("sv", "sv")
            done(A(sv, b[:, :], ACT.Copy), "sv")
            b = bank_of("iq", "iq")
            done(A(iqT, b[:, :], ACT.Copy), "iq")
            b = bank_of("idx", "ik")
            done(A(ikT, b[:, 0:T], ACT.Copy), "ik")
            b = wait_full("iw")
            done(A(iw, b[:, 0:16], ACT.Copy), "iw")

            def decay_exp(lv):
                act.wait_ge(decay_arg_ready, lv)
                A(E_hg[lv % 2], E_hg[lv % 2], ACT.Exp).then_inc(decay_exp_done, 1)

            decay_exp(1)
            decay_exp(2)
            for j in range(2):
                b = bank_of(f"sqk.{j}", "sqk", j)
                done(A((sqT, skT)[j], b[:, :], ACT.Copy), "sqk", j)
            decay_exp(3)
            decay_exp(4)
            for j in range(2):
                b = bank_of(f"hg.{j}", "hg", j)
                A(sg_hg[:, j * 512:(j + 1) * 512], b[:, :], ACT.Sigmoid).then_inc(hg_sig_done, 1)
            decay_exp(5)
            decay_exp(6)
            for j in range(2):
                b = bank_of(f"hi.{j}", "hi", j)
                done(A(v_hg.rearrange("p (t n) -> p t n", t=2)[:, :, j * T:(j + 1) * T],
                       b[:, :].rearrange("p (t n) -> p t n", t=2), ACT.Copy), "hi", j)
            decay_exp(7)
            decay_exp(8)
            b = wait_full("lev", 8, 0)
            done(A(A1_hg, b[:, :], ACT.Copy), "lev", 8, 0)
            for t in range(TT):
                K = (t + 1) * P
                for j in range(4):
                    i = 4 * t + j
                    b = wait_full("sc", t, j)
                    if i >= 2:
                        act.wait_ge(relu_used, i - 1)
                    done(A(relu[i % 2][:, 0:2 * K], b[:, 0:2 * K], ACT.Relu, scale=1.0 / 16), "sc", t, j)
            ahead("hi.1")
            for t in range(TT):
                b = wait_full("hgo", t)
                o = k_hg[:, t * 512:(t + 1) * 512]
                A(o, b[:, :], ACT.Copy)
                for h in range(4):
                    last = A(G_hg[:, (4 * t + h) * P:(4 * t + h + 1) * P], b[:, h * P:(h + 1) * P], ACT.Square,
                             accum_out=ssum[:, 4 * t + h:4 * t + h + 1])
                done(last, "hgo", t)
            square_root(8, 2)
            act.wait_ge(bank_read[bank("cvar")], read("cvar"))
            A(hpad[:, 0:T], hpad[:, 0:T], ACT.Sqrt).then_inc(root_ready, 1)
            act.wait_ge(conv_scaled, 1)
            for c in range(2):
                last = A(conv_d[:, c * T:(c + 1) * T], conv[:, c * T:(c + 1) * T], ACT.Sigmoid)
            last.then_inc(conv_sig_done, 1)
            softmax("dsa", 4, 0)
            for n_ in ("wo0.0", "wo0.1", "wo1.0", "wo1.1"):
                ahead(n_)
            act.wait_ge(x_res_ready, 1)
            rms_squares(2)
            square_root(TT, 4 - 1)
            evacuate("mlp", norm_a, mod[:, 24:32])
            for i in range(8):
                for j in range(2):
                    n = 2 * i + j
                    b = bank_of(f"m1_{i}.{j}", f"m1_{i}", j)
                    if n >= 2:
                        act.wait_ge(hid_split, n - 1)
                    done(A(act_out[n % 2], b[:, :], ACT.Relu), f"m1_{i}", j)
            for i in range(16):
                ahead(f"m2_{i}")
            act.wait_ge(x_res_ready, 2)
            rms_squares(3)
            square_root(TT, 4)
            evacuate("fin", col("fin_w", 0, 8), zero8)
            act.wait_ge(psum_full, full("tr", "fin", 3))
            act.dma_start(lay.rearrange("p (r n) -> p r n", r=5),
                          prow_in[0:5, :].partition_broadcast(P)).then_inc(lay_loaded, 16)
            roots = 4
            base = 4
            for layer in range(2):
                if layer == 0:
                    for e in range(2):
                        b = bank_of(f"cqkv.{e}", "cqkv", e)
                        A(xn[:, :, e * T:(e + 1) * T], b[:, :].rearrange("p (t n) -> p t n", t=2), ACT.Copy)
                        for t in range(TT):
                            last = A(xn[:, t, 512 + e * T:512 + (e + 1) * T], b[:, t * T:(t + 1) * T], ACT.Square,
                                     accum_out=ssum[:, 2 * t + e:2 * t + e + 1])
                        done(last, "cqkv", e)
                    roots += 1
                    square_root(4, roots)
                    for j in range(2):
                        b = bank_of(f"sbq.{j}", "sbq", j)
                        done(A(qT_b[:, j * 512:(j + 1) * 512], b[:, :], ACT.Copy, scale=0.125), "sbq", j)
                    for j in range(2):
                        b = bank_of(f"sbk.{j}", "sbk", j)
                        done(A(kT_b[:, j * 512:(j + 1) * 512], b[:, :], ACT.Copy), "sbk", j)
                    for j in range(2):
                        b = bank_of(f"sbv.{j}", "sbv", j)
                        done(A(v_b.rearrange("p (t n) -> p t n", t=2)[:, :, j * T:(j + 1) * T],
                               b[:, :].rearrange("p (t n) -> p t n", t=2), ACT.Copy), "sbv", j)
                    for j in range(2):
                        b = wait_full("ct", j)
                        for c in range(2):
                            g = col("q_norm" if j == 0 else "kv_norm", c)
                            last = A(fresh[:, (2 * j + c) * T:(2 * j + c + 1) * T], b[:, c * T:(c + 1) * T],
                                     ACT.Copy, scale=g)
                        done(last, "ct", j)
                    for t in range(TT):
                        for n in range(2):
                            m = 512 if n == 0 else 256
                            b = bank_of("uq", "uq", t, n)
                            done(A(qtok[:, t * 768 + n * 512:t * 768 + n * 512 + m], b[:, 0:m], ACT.Copy), "uq", t, n)
                    for j in range(4):
                        b = bank_of("ukv", "uk", j)
                        done(A(kT_a[0:64, j * 512:(j + 1) * 512], b[0:64, :], ACT.Copy), "uk", j)
                    for n in range(2):
                        b = wait_full("uv", n)
                        done(A(v_a.rearrange("p (t n) -> p t n", t=2)[:, :, n * T:(n + 1) * T],
                               b[:, :].rearrange("p (t n) -> p t n", t=2), ACT.Copy), "uv", n)
                    us = units(8)
                    for i in range(len(us) + 2):
                        if i < len(us):
                            K = (us[i][2] + 1) * P
                            e = sb_e[i % 2][:, 0:2 * K]
                            act.wait_ge(bank_read[bank("sb", "L", i)], read("sb", "L", i))
                            link(A(e, unit_logits[i % 4][:, 0:2 * K], ACT.Abs))
                            link(A(e, e, ACT.Exp, scale=-1.0))
                            A(e, e, ACT.Ln, bias=1.0).then_inc(softplus_done, 1)
                        if 0 <= i - 1 < len(us):
                            K = (us[i - 1][2] + 1) * P
                            act.wait_ge(stick_arg_ready, i)
                            L = unit_logits[(i - 1) % 4][:, 0:2 * K]
                            A(L, L, ACT.Exp).then_inc(stick_probs_ready, 1)
                        if i >= 2:
                            transposed("sb", us, i - 2)
                    for j in range(4):
                        b = wait_full("qt", j)
                        done(A(qT_a[0:96, j * 512:(j + 1) * 512], b[0:96, :], ACT.Copy), "qt", j)
                    softmax("mla", 8, base)
                    base += 8
                else:
                    ahead("ff")
                    act.wait_ge(bank_read[bank("ff")], read("ff"))
                    link(A(f_l[0:16, :], f_y[0:16, :], ACT.Abs))
                    link(A(f_l[0:16, :], f_l[0:16, :], ACT.Exp, scale=-1.0))
                    A(f_l[0:16, :], f_l[0:16, :], ACT.Ln, bias=1.0).then_inc(forget_ln_done, 1)
                    for n_, dst, s in [("fq0", qT_c[:, 0:1024], 0.125), ("fq1", qT_c[:, 1024:2048], 0.125),
                                       ("fk0", kT_c[:, 0:1024], 1.0), ("fk1", kT_c[:, 1024:2048], 1.0)]:
                        for j in range(2):
                            b = bank_of(f"{n_}.{j}", n_, j)
                            done(A(dst[:, j * 512:(j + 1) * 512], b[:, :], ACT.Copy, scale=s), n_, j)
                    for n in range(2):
                        for j in range(2):
                            b = bank_of(f"fv{n}.{j}", f"fv{n}", j)
                            c = n * 512 + j * T
                            done(A(v_c.rearrange("p (t n) -> p t n", t=2)[:, :, c:c + T],
                                   b[:, :].rearrange("p (t n) -> p t n", t=2), ACT.Copy), f"fv{n}", j)
                    softmax("fox", 16, base)
                    base += 16
                for i in range(2):
                    for j in range(2):
                        ahead(f"o{layer}_{i}.{j}")
                roots += 1
                square_root(TT, roots)
                evacuate(f"ln1_{layer}", col(f"ln1_g{layer}", 0, 8), col(f"ln1_b{layer}", 0, 8))
                for i in range(11):
                    b = bank_of(f"f13_{layer}_{i}.0", f"f13_{layer}_{i}", 0)
                    if i >= 2:
                        act.wait_ge(bank_read[bank(f"f13_{layer}_{i - 2}", 1)], read(f"f13_{layer}_{i - 2}", 1))
                    A(act_out[i % 2], b[:, :], ACT.Sigmoid).then_inc(silu_sig_done, 1)
                    ahead(f"f13_{layer}_{i}.1")
                for i in range(11):
                    ahead(f"f2_{layer}_{i}")
                roots += 1
                square_root(TT, roots)
                evacuate(f"ln2_{layer}", col(f"ln2_g{layer}", 0, 8), col(f"ln2_b{layer}", 0, 8))
                ahead(f"pp{layer}")
                for n in range(4):
                    ahead(f"pg{layer}_{n // 2}.{n % 2}")
                    key = (f"pg{layer}_{n // 2}", n % 2)
                    act.wait_ge(bank_read[bank(*key)], read(*key))
                    z = xn[:, :, n * T:(n + 1) * T]
                    A(z, z, ACT.Sigmoid).then_inc(ple_sig_done, 1)
                if layer == 0:
                    evacuate("ple", None, None)
                    act.dma_start(lay.rearrange("p (r n) -> p r n", r=5),
                                  prow_in[5:10, :].partition_broadcast(P)).then_inc(lay_loaded, 16)

        @block.gpsimd
        def _(pool):
            step = [0]

            def link(ins):
                step[0] += 1
                ins.then_inc(pool_step, 1)
                pool.wait_ge(pool_step, step[0])

            def remainder(name):
                n, slot = SPLIT_NO[name], TILE_NO[name]
                pool.wait_ge(weights_rounded, n + 1)
                if n >= LO:
                    pool.wait_ge(weights_started, n - LO + 2)
                m = width(name)
                nc.gpsimd.tensor_tensor(w_lo[n % LO][:, 0:m], raw[:, slot % RAW, 0:m],
                                        w_hi[n % HI][:, 0:m].bitcast(F32), ALU.subtract).then_inc(weights_split, 1)

            hp = hpad.rearrange("p (c n) -> p c n", c=2)
            acc = conv.rearrange("p (c n) -> p c n", c=2)

            def tap(j):
                product_ = mixT[:, 4 + 2 * (j % 2):6 + 2 * (j % 2), :]
                w = col("cv_w", 2 * j, 2).unsqueeze(2).to_broadcast([P, 2, T])
                link(nc.gpsimd.tensor_tensor(product_, hp[:, :, j:j + T], w, ALU.mult))
                before = col("cv_b", 0, 2).unsqueeze(2).to_broadcast([P, 2, T]) if j == 0 else acc
                last = nc.gpsimd.tensor_tensor(acc, product_, before, ALU.add)
                if j < 30:
                    link(last)
                else:
                    last.then_inc(conv_done, 1)

            for name in SPLIT[:SPLIT_NO["hg.0"]]:
                remainder(name)
            pool.wait_ge(pcol_loaded, 16)
            pool.wait_ge(bank_read[bank("cu", 0)], read("cu", 0))
            for j in range(31):
                tap(j)
                if j % 2 == 0 and SPLIT_NO["hg.0"] + j // 2 < SPLIT_NO["wo0.0"]:
                    remainder(SPLIT[SPLIT_NO["hg.0"] + j // 2])
            for name in SPLIT[SPLIT_NO["wo0.0"]:]:
                remainder(name)

        @block.vector
        def _(dve):
            step = [0]
            V = nc.vector

            def link(ins):
                step[0] += 1
                ins.then_inc(dve_step, 1)
                dve.wait_ge(dve_step, step[0])

            def wait_full(*key):
                dve.wait_ge(psum_full, full(*key))
                return ps(*key)

            def done(ins, *key):
                ins.then_inc(bank_read[bank(*key)], 1)
                dve.wait_ge(bank_read[bank(*key)], read(*key))

            made = {}

            def own(s):
                made[s.name] = made.get(s.name, 0) + 1
                dve.wait_ge(s, made[s.name])

            def wait_done(*key):
                dve.wait_ge(bank_read[bank(*key)], read(*key))

            def split_input(src, j, base_chunk=0):
                s = slice((base_chunk + 2 * j) * T, (base_chunk + 2 * j + 2) * T)
                link(V.tensor_copy(hT_hi[:, s], src))
                V.tensor_tensor(hT_lo[:, s], src, hT_hi[:, s].bitcast(F32), ALU.subtract).then_inc(input_split, 1)
                own(input_split)

            def split_transposed(stage):
                for j in range(4):
                    wait_done("tr", stage, j)
                    split_input(fresh[:, 2 * j * T:(2 * j + 2) * T], j)

            def split_mixed():
                for j in range(4):
                    split_input(mixT[:, 2 * j:2 * j + 2, :].rearrange("p c n -> p (c n)"), j)

            roots = [0]

            def rstd(width, scale, eps, src):
                V.tensor_scalar(stat[:, 0:width], src, scale, eps, ALU.mult, ALU.add).then_inc(var_ready, 1)
                own(var_ready)
                roots[0] += 1
                dve.wait_ge(root_ready, roots[0] + extra_roots[0])
                link(V.reciprocal(stat[:, 8:8 + width], root[:, 0:width]))

            extra_roots = [0]

            def rms_norm(n):
                dve.wait_ge(squares_summed, n)
                rstd(TT, 1.0 / D, EPS, ssum[:, 0:TT])
                for t in range(TT):
                    last = V.tensor_scalar(xn[:, t, :], x[:, t, :], stat[:, 8 + t:9 + t], None, ALU.mult)
                last.then_inc(xn_ready, 1)
                own(xn_ready)

            def softmax(name, heads, base, bias, scale, c0):
                us = units(heads)
                n = len(us)
                for i in range(n + 3):
                    if i < n:
                        g, par, t = us[i]
                        K = (t + 1) * P
                        m = 2 * (i % 4)
                        b = wait_full(name, "L", i)
                        L = unit_logits[i % 4][:, 0:2 * K].rearrange("p (h k) -> p h k", h=2)
                        if name == "fox":
                            for hh in range(2):
                                h = 4 * g + par + 2 * hh
                                last = V.scalar_tensor_tensor(out=L[:, hh, :], in0=b[:, hh * K:(hh + 1) * K],
                                                              scalar=dtok[:, t * 16 + h:t * 16 + h + 1],
                                                              in1=bias(t), op0=ALU.add, op1=ALU.add)
                        else:
                            last = V.scalar_tensor_tensor(
                                out=L, in0=b[:, 0:2 * K].rearrange("p (h k) -> p h k", h=2), scalar=scale,
                                in1=bias(t).unsqueeze(1).to_broadcast([P, 2, K]), op0=ALU.mult, op1=ALU.add)
                        done(last, name, "L", i)
                        V.tensor_reduce(negmax[:, m:m + 2], L, AX.X, ALU.max, negate=True).then_inc(logits_ready, 1)
                        own(logits_ready)
                    if 0 <= i - 1 < n:
                        t = us[i - 1][2]
                        K = (t + 1) * P
                        m = 2 * ((i - 1) % 4)
                        dve.wait_ge(exp_done, base_exp[0] + i)
                        link(V.reciprocal(rinv[:, m:m + 2], rowsum[:, m:m + 2]))
                        for hh in range(2):
                            L = unit_logits[(i - 1) % 4][:, hh * K:(hh + 1) * K]
                            last = V.tensor_scalar(L, L, rinv[:, m + hh:m + hh + 1], None, ALU.mult)
                        last.then_inc(probs_ready, 1)
                        own(probs_ready)
                    if 0 <= i - 3 < n:
                        unit_output(name, us, i - 3, c0)
                base_exp[0] += n

            base_exp = [0]

            def modulation_columns(u):
                b = wait_full("mod", u)
                done(V.tensor_tensor(h4(lev_tmp[u % 2]), h4(b[:, :]), ident.unsqueeze(1).to_broadcast([P, 4, P]),
                                     ALU.mult), "mod", u)
                m = mod[:, 4 * u:4 * u + 4]
                link(V.tensor_reduce(m, h4(lev_tmp[u % 2]), AX.X, ALU.add))
                link(V.tensor_tensor(m, m, col("ada_b", 4 * u, 4), ALU.add))

            def modulation_row(u, row):
                b = wait_full("mod", u)
                done(V.tensor_tensor(row, b[:, :], row, ALU.add), "mod", u)

            def unit_output(name, us, i, c0):
                g, par, t = us[i]
                b = wait_full(name, "O", i)
                r = par * 64
                done(V.tensor_copy(mixT[r:r + 64, c0 + 2 * g:c0 + 2 * g + 2, t * P:(t + 1) * P],
                                   b[r:r + 64, 0:T].rearrange("p (c n) -> p c n", c=2)), name, "O", i)

            V.memset(avg[:, :], 1.0 / 256)
            V.memset(zero8, 0.0)
            V.memset(hpad, 0.0)
            link(V.memset(ones[:, :], 1.0))
            dve.wait_ge(pcol_loaded, 16)
            V.tensor_tensor(lbw[:, 0:4], col("lb", 0, 4), col("lb", 0, 4), ALU.subtract).then_inc(lb_diff_ready, 1)
            own(lb_diff_ready)
            dve.wait_ge(lb_exp_done, 1)
            link(V.reciprocal(lbw[:, 4:8], lbw[:, 0:4]))
            link(V.tensor_tensor(lbw[:, 0:4], lbw[:, 0:4], lbw[:, 4:8], ALU.mult))
            link(V.tensor_tensor(lb, lbw[:, 0:4], lbw[:, 0:4], ALU.subtract))
            V.tensor_scalar(one_lb, lb, -1.0, 1.0, ALU.mult, ALU.add)
            dve.wait_ge(c_sig_done, 1)
            V.tensor_tensor(csil, csil, col("c", 0, 8), ALU.mult).then_inc(c_ready, 1)
            own(c_ready)
            rms_norm(1)
            dve.wait_ge(const_loaded, 16)
            for u in range(4):
                modulation_columns(u)
            V.scalar_tensor_tensor(out=norm_a, in0=mod[:, 8:16], scalar=1.0, in1=col("mix_w", 0, 8),
                                   op0=ALU.add, op1=ALU.mult).then_inc(norm_coef_ready, 1)
            own(norm_coef_ready)
            split_transposed("mix")
            for j in range(2):
                wait_done("hf", j)
            for h in range(4):
                s = slice(h * T, (h + 1) * T)
                V.tensor_scalar(k_hg[:, s], k_hg[:, s], one_lb[:, h:h + 1], None, ALU.mult)
                last = V.tensor_scalar(G_hg[:, s], G_hg[:, s], one_lb[:, h:h + 1], lb[:, h:h + 1], ALU.mult, ALU.add)
            link(last)
            link(V.tensor_scalar(G_hg, G_hg, TINY, None, ALU.max))
            link(V.tensor_scalar(QK[0], G_hg, LN_SPLIT, 1.0, ALU.mult, ALU.min))
            V.tensor_scalar(G_hg, G_hg, 1.0 / LN_SPLIT, None, ALU.max).then_inc(f_clipped, 1)
            own(f_clipped)
            for j in range(2):
                b = wait_full("hq", j)
                dve.wait_ge(hq_sig_done, j + 1)
                s = slice(j * 512, (j + 1) * 512)
                done(V.scalar_tensor_tensor(out=q_hg[:, s], in0=b[:, :], scalar=P ** -0.5, in1=q_hg[:, s],
                                            op0=ALU.mult, op1=ALU.mult), "hq", j)
            dve.wait_ge(logs_done, 1)
            link(V.tensor_tensor(G_hg, G_hg, QK[0], ALU.add))
            for h in range(4):
                s = slice(h * T, (h + 1) * T)
                last = V.tensor_tensor_scan(E_hg[0][:, s], ones[:, :], G_hg[:, s], 0.0, ALU.mult, ALU.add)
            link(last)
            V.tensor_copy(G_hg, E_hg[0]).then_inc(qk_ready, 1)
            own(qk_ready)

            def halves(a, bsz):
                v = a.rearrange("p (n two b) -> p n two b", two=2, b=bsz)
                return v[:, :, 0, :], v[:, :, 1, :]

            def decay_args(lv):
                bsz = 1 << (lv - 1)
                left, right = halves(G_hg, bsz)
                el, er = halves(E_hg[lv % 2], bsz)
                n = 512 // bsz
                ref = left[:, :, bsz - 1:bsz].to_broadcast([P, n, bsz])
                V.tensor_tensor(el, ref, left, ALU.subtract)
                V.tensor_tensor(er, right, ref, ALU.subtract).then_inc(decay_arg_ready, 1)
                own(decay_arg_ready)

            def decay_factors(lv):
                bsz = 1 << (lv - 1)
                dve.wait_ge(decay_exp_done, lv)
                kl, _ = halves(k_hg, bsz)
                _, qr = halves(q_hg, bsz)
                el, er = halves(E_hg[lv % 2], bsz)
                ol, orr = halves(QK[lv % 2], bsz)
                if lv >= 3:
                    dve.wait_ge(psum_full, full("lev", lv - 2, 1))
                V.tensor_tensor(ol, kl, el, ALU.mult)
                V.tensor_tensor(orr, qr, er, ALU.mult).then_inc(qk_ready, 1)
                own(qk_ready)

            def decay_sum(lv):
                at = CONST["levels"] + (lv - 1) * P
                m = (ident if lv == 0 else const[:, at:at + P]).unsqueeze(1).to_broadcast([P, 4, P])
                for j in range(2):
                    b = wait_full("lev", lv, j)
                    Aj = A_hg[:, j * 512:(j + 1) * 512]
                    dst = Aj if lv == 0 else lev_tmp[j]
                    done(V.tensor_tensor(h4(dst), h4(b[:, :]), m, ALU.mult), "lev", lv, j)
                if lv:
                    for j in range(2):
                        wait_done("lev", lv, j)
                        Aj = A_hg[:, j * 512:(j + 1) * 512]
                        last = V.tensor_tensor(Aj, Aj, lev_tmp[j], ALU.add)
                    if lv == 7:
                        last.then_inc(levels_summed, 1)
                        own(levels_summed)
                    else:
                        link(last)
                else:
                    for j in range(2):
                        wait_done("lev", lv, j)

            decay_args(1)
            decay_args(2)
            wait_done("cu", 1)
            b = wait_full("cu", 0)
            done(V.tensor_tensor(hpad.rearrange("p (c n) -> p c n", c=2)[:, :, 30:286],
                                 b[:, :].rearrange("p (c n) -> p c n", c=2),
                                 conv_d.rearrange("p (c n) -> p c n", c=2), ALU.mult), "cu", 0)
            decay_factors(1)
            for lv in range(2, 9):
                if lv + 1 <= 8:
                    decay_args(lv + 1)
                decay_factors(lv)
                decay_sum(lv - 2)
                if lv == 5:
                    for j in range(2):
                        b = wait_full("hg", j)
                        dve.wait_ge(hg_sig_done, j + 1)
                        for c in range(2):
                            h = 2 * j + c
                            s = slice(h * T, (h + 1) * T)
                            last = V.scalar_tensor_tensor(out=sg_hg[:, s], in0=b[:, c * T:(c + 1) * T],
                                                          scalar=col("onorm", h), in1=sg_hg[:, s],
                                                          op0=ALU.mult, op1=ALU.mult)
                        done(last, "hg", j)
            decay_sum(7)
            wait_done("iw")
            for t in range(TT):
                K = (t + 1) * P
                sc, B = score[t][:, 0:K], bias_of("causal", t)
                for j in range(4):
                    wait_done("sc", t, j)
                    r = relu[(4 * t + j) % 2]
                    for hh in range(2):
                        ins = V.scalar_tensor_tensor(
                            out=sc, in0=r[:, hh * K:(hh + 1) * K], scalar=iw[:, t * 8 + j + 4 * hh:t * 8 + j + 4 * hh + 1],
                            in1=B if j + hh == 0 else sc, op0=ALU.mult, op1=ALU.add)
                        if hh == 1:
                            ins.then_inc(relu_used, 1)
                            own(relu_used)
                        else:
                            link(ins)
                left = score_left[:, 0:K]
                cur = sc
                for r_ in range(TOPK // 8):
                    link(V.max(m8, cur))
                    if r_ < TOPK // 8 - 1:
                        link(V.match_replace(left, m8, cur, -3.0e38))
                        cur = left
                thr = m8[:, 7:8]
                pk = picks[:, 0:K]
                link(V.tensor_scalar(pk, sc, thr, 0.0, ALU.is_gt, ALU.add, accum_out=count[:, 0:1]))
                link(V.tensor_scalar(need[:, 0:1], count[:, 0:1], -1.0, float(TOPK), ALU.mult, ALU.add))
                link(V.tensor_scalar(sc, sc, thr, None, ALU.is_equal))
                link(V.tensor_tensor_scan(left, ones[:, 0:K], sc, 0.0, ALU.mult, ALU.add))
                link(V.scalar_tensor_tensor(out=left, in0=left, scalar=need[:, 0:1], in1=sc,
                                            op0=ALU.is_le, op1=ALU.mult))
                link(V.tensor_tensor(pk, pk, left, ALU.add))
                link(V.tensor_scalar(pk, pk, -1.0, -NEG, ALU.add, ALU.mult))
                link(V.tensor_tensor(sel_bias[t][:, 0:K], pk, B, ALU.add))
            dve.wait_ge(gate_bias_loaded, 32)
            modulation_row(4, rows[:, 1, 0:512])
            modulation_row(5, rows[:, 1, 512:1024])
            for u in range(6, 10):
                modulation_columns(u)
            modulation_row(10, g2_row[:, 0:512])
            modulation_row(11, g2_row[:, 512:1024])
            V.scalar_tensor_tensor(out=norm_a, in0=mod[:, 32:40], scalar=1.0, in1=col("mlp_w", 0, 8),
                                   op0=ALU.add, op1=ALU.mult)
            wait_done("hgo", 0)
            wait_done("hgo", 1)
            rstd(8, 1.0 / P, EPS, ssum[:, 0:8])
            for t in range(TT):
                V.tensor_tensor(h4(q_hg[:, t * 512:(t + 1) * 512]), h4(k_hg[:, t * 512:(t + 1) * 512]),
                                stat[:, 8 + 4 * t:12 + 4 * t].unsqueeze(2).to_broadcast([P, 4, P]),
                                ALU.mult).then_inc(o_normed, 1)
                own(o_normed)
            c2 = lambda a: a.rearrange("p (c n) -> p c n", c=2)
            b = wait_full("cmean")
            done(V.tensor_tensor(c2(conv_d), c2(conv), b[:, 0:T].unsqueeze(1).to_broadcast([P, 2, T]),
                                 ALU.subtract), "cmean")
            wait_done("cmean")
            V.tensor_tensor(conv, conv_d, conv_d, ALU.mult).then_inc(conv_sq_ready, 1)
            own(conv_sq_ready)
            b = wait_full("cvar")
            done(V.tensor_scalar(hpad[:, 0:T], b[:, 0:T], EPS, None, ALU.add), "cvar")
            wait_done("cvar")
            extra_roots[0] += 1
            dve.wait_ge(root_ready, roots[0] + extra_roots[0])
            link(V.reciprocal(hpad[:, T:2 * T], hpad[:, 0:T]))
            link(V.tensor_tensor(c2(conv_d), c2(conv_d), hpad[:, T:2 * T].unsqueeze(1).to_broadcast([P, 2, T]),
                                 ALU.mult))
            for c in range(2):
                s = slice(c * T, (c + 1) * T)
                last = V.tensor_scalar(conv[:, s], conv_d[:, s], col("cv_ln_w", c), col("cv_ln_b", c),
                                       ALU.mult, ALU.add)
            last.then_inc(conv_scaled, 1)
            own(conv_scaled)
            dve.wait_ge(conv_sig_done, 1)
            V.tensor_tensor(mixT[:, 6:8, :], c2(conv), c2(conv_d), ALU.mult).then_inc(conv_out_ready, 1)
            own(conv_out_ready)
            for t in range(TT):
                b = wait_full("hgt", t)
                done(V.tensor_tensor(mixT[:, 0:4, t * P:(t + 1) * P], h4(b[:, :]),
                                     sg_hg.rearrange("p (h n) -> p h n", h=4)[:, :, t * P:(t + 1) * P],
                                     ALU.mult), "hgt", t)
            softmax("dsa", 4, 0, lambda t: sel_bias[t][:, 0:(t + 1) * P], 0.125, 4)

            def gated_residual(keys):
                for n, key in enumerate(keys):
                    b = wait_full(*key)
                    g = gate_tmp[n % 2].rearrange("p (t n) -> p t n", t=2)
                    done(V.tensor_tensor(g, b[:, :].rearrange("p (t n) -> p t n", t=2),
                                         rows[:, 1:2, n * T:(n + 1) * T].to_broadcast([P, TT, T]), ALU.mult), *key)
                    wait_done(*key)
                    xs = x[:, :, n * T:(n + 1) * T]
                    last = V.tensor_tensor(xs, xs, g, ALU.add)
                last.then_inc(x_res_ready, 1)
                own(x_res_ready)

            split_mixed()
            gated_residual([(f"wo{n}", j) for n in range(2) for j in range(2)])
            rms_norm(2)
            split_transposed("mlp")

            for n in range(16):
                key = (f"m1_{n // 2}", n % 2)
                wait_done(*key)
                v = product[n % 2]
                hs = slice(2 * n * T, (2 * n + 2) * T)
                link(V.tensor_tensor(v, act_out[n % 2], act_out[n % 2], ALU.mult))
                link(V.tensor_copy(hid_hi[:, hs], v))
                V.tensor_tensor(hid_lo[:, hs], v, hid_hi[:, hs].bitcast(F32), ALU.subtract).then_inc(hid_split, 1)
                own(hid_split)

            def gated_residual2():
                for i, (t, n) in enumerate([(t, n) for t in range(TT) for n in range(2)]):
                    b = wait_full("m2", t, n)
                    done(V.tensor_tensor(res_tmp[i % 2], b[:, :], g2_row[:, n * 512:(n + 1) * 512], ALU.mult),
                         "m2", t, n)
                    wait_done("m2", t, n)
                    xs = x[:, t, n * 512:(n + 1) * 512]
                    last = V.tensor_tensor(xs, xs, res_tmp[i % 2], ALU.add)
                last.then_inc(x_res_ready, 1)
                own(x_res_ready)

            gated_residual2()
            rms_norm(3)
            dve.wait_ge(rows_loaded, 16)
            for t in range(TT):
                last = V.tensor_tensor(x[:, t, :], xn[:, t, :], rows[:, 0, :], ALU.mult)
            link(last)
            split_transposed("fin")
            base_exp[0] = 4

            def bn_piece(t, n):
                return V.bn_stats(bn[:, (2 * t + n) * 6:(2 * t + n + 1) * 6], x[:, t, n * 512:(n + 1) * 512])

            def add_attention(layer):
                for q in range(4):
                    key = (f"o{layer}_{q // 2}", q % 2)
                    b = wait_full(*key)
                    xs = x[:, :, q * T:(q + 1) * T]
                    done(V.scalar_tensor_tensor(out=xs, in0=xs, scalar=ALPHA,
                                                in1=b[:, :].rearrange("p (t n) -> p t n", t=2),
                                                op0=ALU.mult, op1=ALU.add), *key)
                    if q % 2:
                        for t in range(TT):
                            last = bn_piece(t, q // 2)
                link(last)

            def add_ffn(layer):
                for t in range(TT):
                    for n in range(2):
                        key = ("f2", layer, t, n)
                        b = wait_full(*key)
                        xs = x[:, t, n * 512:(n + 1) * 512]
                        done(V.scalar_tensor_tensor(out=xs, in0=xs, scalar=ALPHA, in1=b[:, :],
                                                    op0=ALU.mult, op1=ALU.add), *key)
                        last = bn_piece(t, n)
                link(last)

            def split_embeddings(layer):
                if layer == 0:
                    dve.wait_ge(p_loaded, 16)
                src = pT[:, layer, :, :].rearrange("p k n -> p (k n)")
                link(V.tensor_copy(hid2_hi[:, 0:2 * T], src))
                V.tensor_tensor(hid2_lo[:, 0:2 * T], src, hid2_hi[:, 0:2 * T].bitcast(F32),
                                ALU.subtract).then_inc(p_split, 1)
                own(p_split)

            def layer_norm(g_row, b_row, stage, layer):
                for t in range(TT):
                    last = V.bn_aggr(mv[:, 2 * t:2 * t + 2], bn[:, 12 * t:12 * t + 12].rearrange("p (a b) -> p a b", a=2))
                link(last)
                rstd(TT, 1.0, EPS_LN, mv[:, 0:4].rearrange("p (t e) -> p t e", e=2)[:, :, 1])
                for t in range(TT):
                    last = V.tensor_scalar(xn[:, t, :], x[:, t, :], mv[:, 2 * t:2 * t + 1], stat[:, 8 + t:9 + t],
                                           ALU.subtract, ALU.mult)
                last.then_inc(xn_ready, 1)
                own(xn_ready)
                if g_row == 2:
                    split_embeddings(layer)
                split_transposed(stage)
                if g_row == 0:
                    dve.wait_ge(lay_loaded, 16 * (layer + 1))
                for t in range(TT):
                    last = V.tensor_tensor(x[:, t, :], xn[:, t, :], lay_row(g_row), ALU.mult)
                link(last)
                for t in range(TT):
                    last = V.tensor_tensor(x[:, t, :], x[:, t, :], lay_row(b_row), ALU.add)
                link(last)

            for layer in range(2):
                if layer == 0:
                    wait_done("cqkv", 0)
                    wait_done("cqkv", 1)
                    rstd(4, 1.0 / 256, EPS, ssum[:, 0:4])
                    for t in range(TT):
                        for e in range(2):
                            s = xn[:, t, e * T:(e + 1) * T]
                            last = V.tensor_scalar(s, s, stat[:, 8 + 2 * t + e:9 + 2 * t + e], None, ALU.mult)
                    last.then_inc(c_normed, 1)
                    own(c_normed)
                    link(V.memset(krtok, 0.0))
                    V.memset(suffix_mask, 1.0)
                    b = wait_full("kr")
                    kraw = rope_tmp[0][:, 0:64]
                    done(V.tensor_copy(kraw, b[:, 0:64]), "kr")
                    wait_done("kr")
                    V.memset(suffix_mask[:, 255:256], 0.0)

                    def rope(x1, x2, o1, o2, cos, sin, t1, t2, t3, t4):
                        V.tensor_tensor(t1, x1, cos, ALU.mult)
                        V.tensor_tensor(t2, x2, sin, ALU.mult)
                        V.tensor_tensor(t3, x1, sin, ALU.mult)
                        link(V.tensor_tensor(t4, x2, cos, ALU.mult))
                        V.tensor_tensor(o1, t1, t2, ALU.subtract)
                        return V.tensor_tensor(o2, t3, t4, ALU.add)

                    cosv = const[:, CONST["cos"]:CONST["cos"] + 32].rearrange("p (t d) -> p t d", t=2)
                    sinv = const[:, CONST["sin"]:CONST["sin"] + 32].rearrange("p (t d) -> p t d", t=2)
                    kv3 = kraw.rearrange("p (t d) -> p t d", t=2)
                    kt3 = krtok.rearrange("p (t d) -> p t d", t=2)
                    tm = [rope_tmp[1][:, 32 * i:32 * i + 32].rearrange("p (t d) -> p t d", t=2) for i in range(4)]
                    rope(kv3[:, :, 0:16], kv3[:, :, 16:32], kt3[:, :, 64:80], kt3[:, :, 80:96], cosv, sinv, *tm)\
                        .then_inc(k_rope_ready, 1)
                    own(k_rope_ready)
                    for j in range(2):
                        wait_done("ct", j)
                        split_input(fresh[:, 2 * j * T:(2 * j + 2) * T], j)
                    for t in range(TT):
                        wait_done("uq", t, 0)
                        wait_done("uq", t, 1)
                        q3 = qtok[:, t * 768:(t + 1) * 768].rearrange("p (h d) -> p h d", h=8)
                        ct = cosv[:, t, :].unsqueeze(1).to_broadcast([P, 8, 16])
                        st = sinv[:, t, :].unsqueeze(1).to_broadcast([P, 8, 16])
                        tm = [rope_tmp[i // 2][:, 128 * (i % 2):128 * (i % 2) + 128].rearrange("p (h d) -> p h d", h=8)
                              for i in range(4)]
                        last = rope(q3[:, :, 64:80], q3[:, :, 80:96], q3[:, :, 64:80], q3[:, :, 80:96], ct, st, *tm)
                        if t == 0:
                            link(last)
                    last.then_inc(q_rope_ready, 1)
                    own(q_rope_ready)
                    b = wait_full("krt")
                    done(V.tensor_copy(kT_a[64:96, :].rearrange("p (h n) -> p h n", h=8),
                                       b[64:96, 0:T].unsqueeze(1).to_broadcast([32, 8, T])), "krt")
                    us = units(8)
                    n = len(us)
                    for i in range(n + 3):
                        if i < n:
                            t = us[i][2]
                            K = (t + 1) * P
                            b = wait_full("sb", "L", i)
                            L = unit_logits[i % 4][:, 0:2 * K].rearrange("p (h k) -> p h k", h=2)
                            done(V.tensor_tensor(L, b[:, 0:2 * K].rearrange("p (h k) -> p h k", h=2),
                                                 bias_of("strict", t).unsqueeze(1).to_broadcast([P, 2, K]), ALU.add),
                                 "sb", "L", i)
                        if 0 <= i - 1 < n:
                            K = (us[i - 1][2] + 1) * P
                            dve.wait_ge(softplus_done, i)
                            e = sb_e[(i - 1) % 2][:, 0:2 * K]
                            L = unit_logits[(i - 1) % 4][:, 0:2 * K]
                            suf = sb_suffix[:, 0:2 * K]
                            link(V.scalar_tensor_tensor(out=e, in0=L, scalar=0.0, in1=e, op0=ALU.max, op1=ALU.add))
                            m0 = 128 if K == 128 else 0
                            link(V.tensor_tensor_scan(suf[:, ::-1], suffix_mask[:, m0:m0 + 2 * K][:, ::-1], e[:, ::-1],
                                                      0.0, ALU.mult, ALU.add))
                            V.tensor_tensor(L, L, suf, ALU.subtract).then_inc(stick_arg_ready, 1)
                            own(stick_arg_ready)
                        if 0 <= i - 3 < n:
                            unit_output("sb", us, i - 3, 4)
                    softmax("mla", 8, 12, lambda t: bias_of("chunk", t), 96 ** -0.5, 0)
                else:
                    V.memset(dT, 0.0)
                    b = wait_full("ff")
                    done(V.tensor_scalar(f_y[0:16, :], b[0:16, 0:T], col("b_f")[0:16, :], None, ALU.add), "ff")
                    wait_done("ff")
                    dve.wait_ge(forget_ln_done, 1)
                    link(V.scalar_tensor_tensor(out=f_y[0:16, :], in0=f_y[0:16, :], scalar=0.0, in1=f_l[0:16, :],
                                                op0=ALU.min, op1=ALU.subtract))
                    V.tensor_tensor_scan(dT[0:16, :], ones[0:16, :], f_y[0:16, :], 0.0, ALU.mult, ALU.add)\
                        .then_inc(dcum_ready, 1)
                    own(dcum_ready)
                    b = wait_full("fd")
                    done(V.tensor_copy(dtok.rearrange("p (t h) -> p t h", t=2),
                                       b[:, 0:T].rearrange("p (t n) -> p t n", t=2)[:, :, 0:16]), "fd")
                    wait_done("fd")
                    softmax("fox", 16, 20, lambda t: bias_of("causal", t), 1.0, 0)
                split_mixed()
                add_attention(layer)
                layer_norm(0, 1, f"ln1_{layer}", layer)
                for i in range(11):
                    b0 = wait_full(f"f13_{layer}_{i}", 0)
                    dve.wait_ge(silu_sig_done, 11 * layer + i + 1)
                    s, v = act_out[i % 2], product[i % 2]
                    done(V.tensor_tensor(s, b0[:, :], s, ALU.mult), f"f13_{layer}_{i}", 0)
                    b1 = wait_full(f"f13_{layer}_{i}", 1)
                    done(V.tensor_tensor(v, b1[:, :], s, ALU.mult), f"f13_{layer}_{i}", 1)
                    hs = slice(2 * i * T, (2 * i + 2) * T)
                    link(V.tensor_copy(hid2_hi[:, hs], v))
                    V.tensor_tensor(hid2_lo[:, hs], v, hid2_hi[:, hs].bitcast(F32), ALU.subtract)\
                        .then_inc(hid_split, 1)
                    own(hid_split)
                add_ffn(layer)
                layer_norm(2, 3, f"ln2_{layer}", layer)
                for n in range(4):
                    key = (f"pg{layer}_{n // 2}", n % 2)
                    b = wait_full(*key)
                    done(V.tensor_tensor(xn[:, :, n * T:(n + 1) * T], b[:, :].rearrange("p (t n) -> p t n", t=2),
                                         lay_row(4)[:, n * T:(n + 1) * T].unsqueeze(1).to_broadcast([P, TT, T]),
                                         ALU.add), *key)
                for n in range(4):
                    dve.wait_ge(ple_sig_done, 4 * layer + n + 1)
                    b = wait_full("pp", layer, n)
                    z = xn[:, :, n * T:(n + 1) * T]
                    done(V.tensor_tensor(z, b[:, :].rearrange("p (t n) -> p t n", t=2), z, ALU.mult), "pp", layer, n)
                    xs = x[:, :, n * T:(n + 1) * T]
                    last = V.tensor_tensor(xs, xs, z, ALU.add)
                if layer == 0:
                    last.then_inc(xn_ready, 1)
                    own(xn_ready)
                    split_transposed("ple")
                else:
                    last.then_inc(x_done, 1)
                    own(x_done)


def _kn(w):
    k, n = w.shape
    return w.reshape(k // P, P, n).transpose(1, 0, 2).reshape(P, -1)


def _stream(i):
    import numpy as np
    parts = {}

    def halves(name, w):
        for j in range(2):
            parts[f"{name}.{j}"] = _kn(w[:, j * T:(j + 1) * T])

    def block(w, j):
        return w[:, j * 512:(j + 1) * 512]

    for j in range(N_ADA):
        parts[f"ada{j}"] = _kn(i["ada_w"][0][:, j * T:(j + 1) * T])
    w = i["w_in"][0]
    for name, a in [("hq", 0), ("hf", 512), ("hi", 1024), ("hg", 1536), ("sqk", 2048), ("cu", 3112)]:
        halves(name, w[:, a:a + 512])
    parts["sv"], parts["iq"] = _kn(w[:, 2560:2816]), _kn(w[:, 2816:3072])
    parts["idx"] = _kn(np.concatenate([w[:, 3072:3104]] * 4 + [w[:, 3104:3112]], 1))
    for j in range(2):
        halves(f"wo{j}", block(i["w_out"][0], j))
        halves(f"o0_{j}", block(i["a_w_out_2"][0], j))
        halves(f"o1_{j}", block(i["c_w_out_2"][0], j))
    for j in range(8):
        halves(f"m1_{j}", block(i["mlp_w1"][0], j))
    for j in range(16):
        parts[f"m2_{j}"] = _kn(i["mlp_w2"][0][j * T:(j + 1) * T, :])
    a = i["a_w_in_2"][0]
    halves("cqkv", a[:, 0:512])
    parts["kr"] = _kn(a[:, 512:544])
    for j, name in enumerate(("sbq", "sbk", "sbv")):
        halves(name, block(a[:, 544:], j))
    parts["uq"] = _kn(i["a_w_uq_2"][0])
    ukv = i["a_w_ukv_2"][0].reshape(T, 8, 2, 64)
    parts["ukv"] = _kn(np.concatenate([ukv[:, :, j, :].reshape(T, 512) for j in range(2)], 1))
    c = i["c_w_in_2"][0]
    for j in range(2):
        halves(f"fq{j}", block(c, j))
        halves(f"fk{j}", block(c[:, D:], j))
        halves(f"fv{j}", block(c[:, 2 * D:], j))
    parts["ff"] = _kn(c[:, 3 * D:3 * D + 16])
    for l in range(2):
        w1, w3, w2 = i["ffn_w1_2"][l], i["ffn_w3_2"][l], i["ffn_w2_2"][l]
        for j in range(11):
            s = slice(j * T, (j + 1) * T)
            parts[f"f13_{l}_{j}.0"], parts[f"f13_{l}_{j}.1"] = _kn(w1[:, s]), _kn(w3[:, s])
            parts[f"f2_{l}_{j}"] = _kn(w2[s, :])
        for j in range(2):
            halves(f"pg{l}_{j}", block(i["ple_w_gate_2"][l], j))
        parts[f"pp{l}"] = _kn(i["ple_w_proj_2"][l])
    out = np.zeros((len(STREAM), P, TILE), np.float32)
    for n, name in enumerate(STREAM):
        t = parts[name]
        assert t.shape[1] == width(name), name
        out[n, :, 0:t.shape[1]] = t
    return out


def _constant_array():
    import numpy as np
    c = np.zeros((P, N_CONST), np.float32)
    q, s = np.arange(P)[:, None], np.arange(P)[None, :]

    def put(name, a, at=0):
        c[:, CONST[name] + at:CONST[name] + at + a.shape[1]] = a

    put("ident", (q == s).astype(np.float32))
    put("causal", np.where(s <= q, 0.0, NEG), P)
    put("strict", np.where(s < q, 0.0, NEG), P)
    put("chunk", np.where(s // 64 <= q // 64, 0.0, NEG), P)
    for l, b in enumerate(LEVELS):
        m = (q // (2 * b) == s // (2 * b)) & (q // b % 2 == 0) & (s // b % 2 == 1)
        put("levels", m.astype(np.float32), l * P)
    inv = (1.0 / (np.float32(10000.0) ** (np.arange(0, 32, 2, dtype=np.float32) / np.float32(32)))).astype(np.float32)
    ang = np.arange(T, dtype=np.float32)[:, None] * inv[None, :]
    put("cos", np.cos(ang).reshape(2, P, 16).transpose(1, 0, 2).reshape(P, 32))
    put("sin", np.sin(ang).reshape(2, P, 16).transpose(1, 0, 2).reshape(P, 32))
    put("negsel", -(q == s)[:, 0:16].astype(np.float32))
    return c


def kernel(**inputs):
    import numpy as np
    import concourse.bacc as bacc
    from concourse.bass_utils import run_bass_kernel_spmd

    i = {k: np.asarray(v) for k, v in inputs.items()}
    pcol = np.zeros((P, N_PCOL), np.float32)

    def put(name, v):
        v = np.asarray(v)
        pcol[:, PCOL[name]:PCOL[name] + v.size // P] = v.reshape(-1, P).T

    put("c", i["c"][0])
    put("ada_b", i["ada_b"][0])
    put("mix_w", i["norm_mix_w"][0])
    put("mlp_w", i["norm_mlp_w"][0])
    put("lb", i["hg_lb_logits"][0])
    put("onorm", i["hg_onorm_w"][0])
    put("cv_b", i["cv_b"][0])
    put("cv_ln_w", i["cv_ln_w"][0])
    put("cv_ln_b", i["cv_ln_b"][0])
    put("cv_w", i["cv_w"][0])
    put("fin_w", i["final_norm_w"])
    put("q_norm", i["a_q_norm_2"][0])
    put("kv_norm", i["a_kv_norm_2"][0])
    for l in range(2):
        for n in ("ln1_g", "ln1_b", "ln2_g", "ln2_b"):
            put(f"{n}{l}", i[f"{n}_2"][l])
    pcol[0:16, PCOL["b_f"]] = i["c_b_f_2"][0]
    prow = np.stack([i[f"{n}_2"][l] for l in range(2) for n in ("ln1_g", "ln1_b", "ln2_g", "ln2_b", "ple_b_gate")]
                    + [i["final_norm_w"]] + [i["ada_b"][0][j * D:(j + 1) * D] for j in (2, 5)])
    pT = np.concatenate([_kn(np.ascontiguousarray(i["p_2"][l, 0].T)) for l in range(2)], 1)
    arrays = {
        "x": i["x"], "wstream": _stream(i), "pcol": pcol,
        "prow": np.ascontiguousarray(prow), "const": _constant_array(), "p": np.ascontiguousarray(pT),
    }
    nc = bacc.Bacc("TRN2", target_bir_lowering=False, num_devices=1)
    args = [nc.dram_tensor(n, a.shape, F32, kind="ExternalInput").ap() for n, a in arrays.items()]
    out = nc.dram_tensor("out", (1, T, D), F32, kind="ExternalOutput").ap()
    build(nc, *args, out)
    r = run_bass_kernel_spmd(nc, [arrays], core_ids=[0])
    return r.results[0]["out"]
```
